# Optimizing a Trainium2 kernel written in Bass

```python
import math
import jax, jax.numpy as jnp
from jax import lax
import numpy as np

D_MODEL = 1024
BATCH = 1
SEQ = 256
DEPTH = 1
DEC_BATCH = 8
DEC_SEQ = 1
PAST_LEN = 2048
PAGE_SIZE = 128

N_ATTN_HEADS = 8
ATTN_HEAD_DIM = 64
ATTN_WIDTH = N_ATTN_HEADS * ATTN_HEAD_DIM
MOBA_BLOCK = 256
MOBA_TOPK = 3
Q_BLOCK = 128
N_BUCKETS = 32
MAX_DISTANCE = 128
N_M_HEADS = 4
M_HEAD_DIM = 128
M_WIDTH = N_M_HEADS * M_HEAD_DIM
CONV_WIDTH = 4
M_CHUNK = 128
MIX_WIDTH = ATTN_WIDTH + M_WIDTH
PROJ_SIZES = (ATTN_WIDTH,) * 3 + (M_WIDTH,) * 4 + (N_M_HEADS,) * 2
PROJ_WIDTH = sum(PROJ_SIZES)
PROJ_OFFSETS = tuple(sum(PROJ_SIZES[:i + 1]) for i in range(len(PROJ_SIZES) - 1))
N_KEYS = 128
N_EXPERTS = N_KEYS * N_KEYS
PEER_HEADS = 8
PEER_KEY_DIM = 256
PEER_TOPK = 16
PEER_ROWS = 256
LN_EPS = 1e-5
ALPHA = (2.0 * DEPTH) ** 0.25
BETA = (8.0 * DEPTH) ** -0.25

kernel_name = 'hymba_moba_mlstm_peer_step'

def standardize(x):
    xf = x.astype(jnp.float32)
    mu = jnp.mean(xf, -1, keepdims=True)
    var = jnp.mean(jnp.square(xf - mu), -1, keepdims=True)
    return (xf - mu) * lax.rsqrt(var + LN_EPS)

def layer_norm(x, gain, bias):
    return (standardize(x) * gain + bias).astype(x.dtype)

def t5_bucket(dist):
    max_exact = N_BUCKETS // 2
    d = jnp.maximum(dist, 0)
    far = max_exact + (jnp.log(jnp.maximum(d, 1).astype(jnp.float32) / max_exact)
                       / math.log(MAX_DISTANCE / max_exact) * (N_BUCKETS - max_exact)).astype(jnp.int32)
    return jnp.where(d < max_exact, d, jnp.minimum(far, N_BUCKETS - 1))

def head_bias(dist, head_idx, table):
    flat = jnp.transpose(table).reshape(-1)
    return flat[head_idx * N_BUCKETS + t5_bucket(dist)].astype(jnp.float32)

def moba_prompt(q, k, v, table):
    B, S, H, dh = q.shape
    scale = dh ** -0.5
    nb = -(-S // MOBA_BLOCK)
    nbs = max(nb, MOBA_TOPK)
    pad = nbs * MOBA_BLOCK - S
    kp = jnp.pad(k, ((0, 0), (0, pad), (0, 0), (0, 0)))
    vp = jnp.pad(v, ((0, 0), (0, pad), (0, 0), (0, 0)))
    kblk = kp.reshape(B, nbs, MOBA_BLOCK, H, dh).transpose(0, 3, 1, 2, 4)
    vblk = vp.reshape(B, nbs, MOBA_BLOCK, H, dh).transpose(0, 3, 1, 2, 4)
    kmean = jnp.mean(kblk.astype(jnp.float32), axis=3)
    qh = q.transpose(0, 2, 1, 3)
    nqb = S // Q_BLOCK
    heads = jnp.arange(H)
    offs = jnp.arange(MOBA_BLOCK)
    take = jax.vmap(lambda t, ix: t[ix])

    def one(i):
        b = i // nqb
        s0 = (i % nqb) * Q_BLOCK
        ob = s0 // MOBA_BLOCK
        qi = lax.dynamic_slice_in_dim(qh[b], s0, Q_BLOCK, axis=1).astype(jnp.float32)
        kb, vb = kblk[b], vblk[b]
        gate = jnp.einsum('hqd,hnd->hqn', qi, kmean[b])
        gate = jnp.where(jnp.arange(nbs) < ob, gate, -jnp.inf)
        _, sel = lax.top_k(gate, MOBA_TOPK)
        valid = sel < ob
        k_sel = take(kb, sel)
        v_sel = take(vb, sel)
        k_own = lax.dynamic_index_in_dim(kb, ob, axis=1, keepdims=False)
        v_own = lax.dynamic_index_in_dim(vb, ob, axis=1, keepdims=False)
        q_pos = s0 + jnp.arange(Q_BLOCK)
        sel_pos = sel[..., None] * MOBA_BLOCK + offs
        own_pos = ob * MOBA_BLOCK + offs
        l_sel = (jnp.einsum('hqd,hqjrd->hqjr', qi, k_sel) * scale
                 + head_bias(q_pos[:, None, None] - sel_pos, heads[:, None, None, None], table))
        l_sel = jnp.where(valid[..., None], l_sel, -jnp.inf)
        l_own = (jnp.einsum('hqd,hrd->hqr', qi, k_own) * scale
                 + head_bias(q_pos[:, None] - own_pos[None, :], heads[:, None, None], table))
        l_own = jnp.where(own_pos[None, :] <= q_pos[:, None], l_own, -jnp.inf)
        nsel = MOBA_TOPK * MOBA_BLOCK
        p = jax.nn.softmax(jnp.concatenate([l_sel.reshape(H, Q_BLOCK, nsel), l_own], -1), axis=-1)
        p_sel = p[..., :nsel].reshape(H, Q_BLOCK, MOBA_TOPK, MOBA_BLOCK)
        return (jnp.einsum('hqjr,hqjrd->hqd', p_sel, v_sel)
                + jnp.einsum('hqr,hrd->hqd', p[..., nsel:], v_own))

    out = lax.map(one, jnp.arange(B * nqb))
    return out.reshape(B, nqb, H, Q_BLOCK, dh).transpose(0, 1, 3, 2, 4).reshape(B, S, H * dh)

def moba_sample(q, k, v, cache_k, cache_v, page_table, table):
    DB, T, H, dh = q.shape
    scale = dh ** -0.5
    ppb = MOBA_BLOCK // PAGE_SIZE
    nfp = PAST_LEN // MOBA_BLOCK
    r = PAST_LEN - nfp * MOBA_BLOCK
    qf = q.astype(jnp.float32)
    heads = jnp.arange(H)
    q_pos = PAST_LEN + jnp.arange(T)
    logits, values, specs = [], [], []
    if nfp > 0:
        kt = min(MOBA_TOPK, nfp)
        page_sum = jnp.sum(cache_k.astype(jnp.float32), axis=1)
        kmean = page_sum[page_table[:, :nfp * ppb]].reshape(DB, nfp, ppb, H, dh).sum(2) / MOBA_BLOCK
        gate = jnp.einsum('bthd,bnhd->bhtn', qf, kmean)
        _, sel = lax.top_k(gate, kt)
        lpage = sel[..., None] * ppb + jnp.arange(ppb)
        phys = page_table[jnp.arange(DB)[:, None, None, None, None], lpage]
        rows = jnp.arange(PAGE_SIZE)
        hsel = heads[None, :, None, None, None, None]
        nsel = kt * MOBA_BLOCK
        k_sel = cache_k[phys[..., None], rows, hsel].reshape(DB, H, T, nsel, dh)
        v_sel = cache_v[phys[..., None], rows, hsel].reshape(DB, H, T, nsel, dh)
        sel_pos = (lpage[..., None] * PAGE_SIZE + rows).reshape(DB, H, T, nsel)
        logits.append(jnp.einsum('bthd,bhtkd->bhtk', qf, k_sel) * scale
                      + head_bias(q_pos[:, None] - sel_pos, heads[None, :, None, None], table))
        values.append(v_sel)
        specs.append('bhtk,bhtkd->bthd')
    if r > 0:
        own = page_table[:, nfp * ppb:]
        k_own = cache_k[own].reshape(DB, r, H, dh)
        v_own = cache_v[own].reshape(DB, r, H, dh)
        own_pos = nfp * MOBA_BLOCK + jnp.arange(r)
        logits.append(jnp.einsum('bthd,bkhd->bhtk', qf, k_own) * scale
                      + head_bias(q_pos[:, None] - own_pos[None, :], heads[:, None, None], table))
        values.append(v_own)
        specs.append('bhtk,bkhd->bthd')
    l_new = (jnp.einsum('bthd,bkhd->bhtk', qf, k) * scale
             + head_bias(q_pos[:, None] - q_pos[None, :], heads[:, None, None], table))
    logits.append(jnp.where(q_pos[None, :] <= q_pos[:, None], l_new, -jnp.inf))
    values.append(v)
    specs.append('bhtk,bkhd->bthd')
    p = jax.nn.softmax(jnp.concatenate(logits, -1), axis=-1)
    bounds = np.cumsum([0] + [t.shape[-1] for t in logits]).tolist()
    out = sum(jnp.einsum(spec, p[..., bounds[j]:bounds[j + 1]], val)
              for j, (spec, val) in enumerate(zip(specs, values)))
    return out.reshape(DB, T, H * dh)

def causal_conv(x, state, w, b):
    xp = jnp.concatenate([state.astype(x.dtype), x], axis=1)
    L = x.shape[1]
    y = sum(xp[:, j:j + L] * w[j] for j in range(CONV_WIDTH)) + b
    return jax.nn.silu(y), xp[:, -(CONV_WIDTH - 1):]

def mlstm_chunk(state, q, k, v, i_t, logf):
    C, n, m = state
    L = q.shape[2]
    b = jnp.cumsum(logf, axis=-1)
    causal = jnp.tril(jnp.ones((L, L), bool))
    D = jnp.where(causal, b[..., :, None] - b[..., None, :] + i_t[..., None, :], -jnp.inf)
    inter = b + m[..., None]
    m_t = jnp.maximum(inter, jnp.max(D, -1))
    w_inter = jnp.exp(inter - m_t)
    s = jnp.einsum('bhtd,bhsd->bhts', q, k) * jnp.exp(D - m_t[..., None])
    num = w_inter[..., None] * jnp.einsum('bhvk,bhtk->bhtv', C, q) + jnp.einsum('bhts,bhsv->bhtv', s, v)
    den = w_inter * jnp.einsum('bhk,bhtk->bht', n, q) + jnp.sum(s, -1)
    h = num / jnp.maximum(jnp.abs(den), jnp.exp(-m_t))[..., None]
    g = b[..., -1:] - b + i_t
    m_new = jnp.maximum(b[..., -1] + m, jnp.max(g, -1))
    wc = jnp.exp(b[..., -1] + m - m_new)
    ws = jnp.exp(g - m_new[..., None])
    C_new = wc[..., None, None] * C + jnp.einsum('bhs,bhsv,bhsk->bhvk', ws, v, k)
    n_new = wc[..., None] * n + jnp.einsum('bhs,bhsk->bhk', ws, k)
    return (C_new, n_new, m_new), h

def mlstm_mixer(qk_raw, vm, om, ig, fg, C, n, m, conv_state, conv_w, conv_b, b_gate):
    B, L, _ = vm.shape
    qk, new_conv = causal_conv(qk_raw, conv_state, conv_w, conv_b)
    heads = lambda t: t.reshape(B, L, N_M_HEADS, M_HEAD_DIM).transpose(0, 2, 1, 3).astype(jnp.float32)
    q = heads(qk[..., :M_WIDTH])
    k = heads(qk[..., M_WIDTH:]) * (M_HEAD_DIM ** -0.5)
    v = heads(vm)
    i_t = (ig + b_gate[:N_M_HEADS]).astype(jnp.float32).transpose(0, 2, 1)
    logf = jax.nn.log_sigmoid((fg + b_gate[N_M_HEADS:]).astype(jnp.float32)).transpose(0, 2, 1)
    chunk = M_CHUNK if L % M_CHUNK == 0 else L
    nc = L // chunk

    def to_chunks(t):
        return jnp.moveaxis(t.reshape(t.shape[:2] + (nc, chunk) + t.shape[3:]), 2, 0)

    init = (C.astype(jnp.float32), n.astype(jnp.float32), m.astype(jnp.float32))
    (C, n, m), h = lax.scan(lambda st, xs: mlstm_chunk(st, *xs), init,
                            tuple(to_chunks(t) for t in (q, k, v, i_t, logf)))
    h = jnp.moveaxis(h, 0, 2).reshape(B, N_M_HEADS, L, M_HEAD_DIM).transpose(0, 2, 1, 3).reshape(B, L, M_WIDTH)
    return jax.nn.sigmoid(om.astype(jnp.float32)) * h, C, n, m, new_conv

def peer_rows(h, w_query, sub_keys, expert_u, expert_v):
    R = h.shape[0]
    qry = (h @ w_query).astype(jnp.float32).reshape(R, PEER_HEADS, 2, PEER_KEY_DIM // 2)
    half = jnp.einsum('rpsd,snd->rpsn', qry, sub_keys.astype(jnp.float32))
    half_s, half_i = lax.top_k(half, PEER_TOPK)
    n_cand = PEER_TOPK * PEER_TOPK
    cand_s = (half_s[:, :, 0, :, None] + half_s[:, :, 1, None, :]).reshape(R, PEER_HEADS, n_cand)
    cand_i = (half_i[:, :, 0, :, None] * N_KEYS + half_i[:, :, 1, None, :]).reshape(R, PEER_HEADS, n_cand)
    best_s, best_j = lax.top_k(cand_s, PEER_TOPK)
    idx = jnp.take_along_axis(cand_i, best_j, axis=-1)
    g = jax.nn.softmax(best_s, axis=-1)
    act = jax.nn.gelu(jnp.einsum('rd,rpkd->rpk', h, expert_u[idx]).astype(jnp.float32))
    return jnp.einsum('rpk,rpkd->rd', (g * act).astype(h.dtype), expert_v[idx])

def peer(h, w_query, sub_keys, expert_u, expert_v):
    R, Dm = h.shape
    rb = min(PEER_ROWS, R)
    nrb = -(-R // rb)
    hp = jnp.pad(h, ((0, nrb * rb - R), (0, 0))).reshape(nrb, rb, Dm)
    out = lax.map(lambda t: peer_rows(t, w_query, sub_keys, expert_u, expert_v), hp)
    return out.reshape(nrb * rb, Dm)[:R]

def setup_inputs(seed: int = 0) -> dict:
    key = jax.random.key(seed)
    ks = iter(jax.random.split(key, 40))
    f32 = jnp.float32

    def nrm(shape, s=1.0):
        return s * jax.random.normal(next(ks), shape, f32)

    n_pages = PAST_LEN // PAGE_SIZE
    used = DEC_BATCH * n_pages
    n_phys = used + max(1, used // 4)
    page_table = jax.random.permutation(next(ks), n_phys)[:used].reshape(DEC_BATCH, n_pages).astype(jnp.int32)
    cache_shape = (DEPTH, n_phys, PAGE_SIZE, N_ATTN_HEADS, ATTN_HEAD_DIM)
    return {
        'x_prompt': nrm((BATCH, SEQ, D_MODEL)),
        'x_sample': nrm((DEC_BATCH, DEC_SEQ, D_MODEL)),
        'cache_k': nrm(cache_shape),
        'cache_v': nrm(cache_shape),
        'page_table': page_table,
        'state_C': nrm((DEPTH, DEC_BATCH, N_M_HEADS, M_HEAD_DIM, M_HEAD_DIM)),
        'state_n': nrm((DEPTH, DEC_BATCH, N_M_HEADS, M_HEAD_DIM)),
        'state_m': nrm((DEPTH, DEC_BATCH, N_M_HEADS), 0.5),
        'state_conv': nrm((DEPTH, DEC_BATCH, CONV_WIDTH - 1, 2 * M_WIDTH)),
        'c_prompt': nrm((BATCH, D_MODEL)),
        'c_sample': nrm((DEC_BATCH, D_MODEL)),
        'rel_bias_table': nrm((N_BUCKETS, N_ATTN_HEADS), 0.3),
        'w_ada': nrm((DEPTH, D_MODEL, 6 * D_MODEL), D_MODEL ** -0.5),
        'b_ada': nrm((DEPTH, 6 * D_MODEL), 0.02),
        'w_in': nrm((DEPTH, D_MODEL, PROJ_WIDTH), D_MODEL ** -0.5),
        'b_gate': jnp.concatenate([nrm((DEPTH, N_M_HEADS), 0.1), 3.0 + nrm((DEPTH, N_M_HEADS), 0.5)], -1),
        'conv_w': nrm((DEPTH, CONV_WIDTH, 2 * M_WIDTH), 0.5),
        'conv_b': nrm((DEPTH, 2 * M_WIDTH), 0.02),
        'beta_attn': 1.0 + nrm((DEPTH, ATTN_WIDTH), 0.05),
        'beta_mlstm': 1.0 + nrm((DEPTH, M_WIDTH), 0.05),
        'w_out': nrm((DEPTH, MIX_WIDTH, D_MODEL), BETA * MIX_WIDTH ** -0.5),
        'ln1_g': 1.0 + nrm((DEPTH, D_MODEL), 0.05),
        'ln1_b': nrm((DEPTH, D_MODEL), 0.02),
        'w_query': nrm((DEPTH, D_MODEL, PEER_HEADS * PEER_KEY_DIM), D_MODEL ** -0.5),
        'sub_keys': nrm((DEPTH, 2, N_KEYS, PEER_KEY_DIM // 2), (PEER_KEY_DIM // 2) ** -0.5),
        'expert_u': nrm((DEPTH, N_EXPERTS, D_MODEL), D_MODEL ** -0.5),
        'expert_v': nrm((DEPTH, N_EXPERTS, D_MODEL), BETA * PEER_HEADS ** -0.5),
        'ln2_g': 1.0 + nrm((DEPTH, D_MODEL), 0.05),
        'ln2_b': nrm((DEPTH, D_MODEL), 0.02),
    }

def reference(x_prompt, x_sample, cache_k, cache_v, page_table, state_C, state_n, state_m, state_conv,
              c_prompt, c_sample, rel_bias_table, w_ada, b_ada, w_in, b_gate, conv_w, conv_b,
              beta_attn, beta_mlstm, w_out, ln1_g, ln1_b, w_query, sub_keys, expert_u, expert_v,
              ln2_g, ln2_b):
    f32 = jnp.float32

    def layer(l, x, c, mixer):
        sh1, sc1, g1, sh2, sc2, g2 = jnp.split((jax.nn.silu(c) @ w_ada[l] + b_ada[l])[:, None, :], 6, axis=-1)
        h = standardize(x) * (1.0 + sc1) + sh1
        parts = jnp.split(h @ w_in[l], PROJ_OFFSETS, axis=-1)
        attn, mem, new_state = mixer(*parts)
        mixed = jnp.concatenate([attn * beta_attn[l], mem * beta_mlstm[l]], axis=-1).astype(x.dtype)
        x = layer_norm(ALPHA * x + g1 * (mixed @ w_out[l]), ln1_g[l], ln1_b[l])
        h2 = (standardize(x) * (1.0 + sc2) + sh2).astype(x.dtype)
        f = peer(h2.reshape(-1, D_MODEL), w_query[l], sub_keys[l], expert_u[l], expert_v[l]).reshape(x.shape)
        x = layer_norm(ALPHA * x + g2 * f, ln2_g[l], ln2_b[l])
        return x, new_state

    def prompt_mixer(l):
        def mix(aq, ak, av, mq, mk, mv, mo, mi, mf):
            B, S, _ = aq.shape
            split_heads = lambda t: t.reshape(B, S, N_ATTN_HEADS, ATTN_HEAD_DIM)
            k, v = split_heads(ak), split_heads(av)
            attn = moba_prompt(split_heads(aq), k, v, rel_bias_table)
            mem, C, n, m, conv = mlstm_mixer(
                jnp.concatenate([mq, mk], -1), mv, mo, mi, mf,
                jnp.zeros((B, N_M_HEADS, M_HEAD_DIM, M_HEAD_DIM), f32), jnp.zeros((B, N_M_HEADS, M_HEAD_DIM), f32),
                jnp.zeros((B, N_M_HEADS), f32), jnp.zeros((B, CONV_WIDTH - 1, 2 * M_WIDTH), mq.dtype),
                conv_w[l], conv_b[l], b_gate[l])
            return attn, mem, (k, v, C, n, m, conv)
        return mix

    def sample_mixer(l):
        def mix(aq, ak, av, mq, mk, mv, mo, mi, mf):
            DB, T, _ = aq.shape
            split_heads = lambda t: t.reshape(DB, T, N_ATTN_HEADS, ATTN_HEAD_DIM)
            k, v = split_heads(ak), split_heads(av)
            attn = moba_sample(split_heads(aq), k, v, cache_k[l], cache_v[l], page_table, rel_bias_table)
            mem, C, n, m, conv = mlstm_mixer(
                jnp.concatenate([mq, mk], -1), mv, mo, mi, mf,
                state_C[l], state_n[l], state_m[l], state_conv[l], conv_w[l], conv_b[l], b_gate[l])
            return attn, mem, (k, v, C, n, m, conv)
        return mix

    xp, xs = x_prompt, x_sample
    new_p, new_s = [], []
    for l in range(DEPTH):
        xp, st = layer(l, xp, c_prompt, prompt_mixer(l))
        new_p.append(st)
        xs, st = layer(l, xs, c_sample, sample_mixer(l))
        new_s.append(st)

    def stack(states, i):
        return jnp.stack([s[i] for s in states])

    return (xp, xs,
            stack(new_p, 0), stack(new_p, 1), stack(new_p, 2), stack(new_p, 3), stack(new_p, 4), stack(new_p, 5),
            stack(new_s, 0), stack(new_s, 1), stack(new_s, 2), stack(new_s, 3), stack(new_s, 4), stack(new_s, 5))


_drawn_inputs = setup_inputs


def setup_inputs(seed=0):
    import zlib

    import numpy as np

    out = dict(_drawn_inputs(seed))
    spreads = {}
    factors = {'cache_k': 3.097,
     'cache_v': 2.932,
     'rel_bias_table': 3.451,
     'beta_attn': 6.421,
     'beta_mlstm': 2.801,
     'ln2_b': 2.931}
    for name, (base, spread) in spreads.items():
        noise = np.random.default_rng([zlib.crc32(name.encode()), seed]).standard_normal(out[name].shape)
        drawn = base * np.exp(spread * noise) if base else spread * noise
        out[name] = __import__('jax').numpy.asarray(drawn.astype(out[name].dtype))
    for name, factor in factors.items():
        out[name] = (out[name] * factor).astype(out[name].dtype)
    return out
```

```python
from contextlib import ExitStack, contextmanager

import numpy as np

import concourse.bass as bass
from concourse import mybir

F32 = mybir.dt.float32
U32 = mybir.dt.uint32
I32 = mybir.dt.int32
ALU = mybir.AluOpType
ACT = mybir.ActivationFunctionType
AX = mybir.AxisListType.X

P = 128
DM = 1024
KT = DM // P
SEQ = 256
NT = SEQ // P
NB = 8
R = SEQ + NB
AH, AD = 8, 64
AW = AH * AD
MH, MD = 4, 128
MW = MH * MD
NPG = 16
PG = 128
NBLK = 8
TOPB = 3
NBUCK = 32
CW = 4
PH = 8
PK = 16
NK = 128
N = 512
ALPHA = 2.0 ** 0.25
SC_A = AD ** -0.5
SC_M = MD ** -0.5
EPS = 1e-5
NEG = -1e30
GC = 0.7978845608028654
RING = 4
RPITCH = 384
UR = 8


def constants():
    eye = np.eye(P, dtype=np.float32)
    s = np.arange(P)
    upto = (s[:, None] <= s[None, :]).astype(np.float32)
    past_t = np.where(s[None, :] <= s[:, None], 0.0, NEG)
    past_s = np.where(s[:, None] <= s[None, :], 0.0, NEG)
    head_sum = np.zeros((P, NB))
    for p in range(AH * NB):
        head_sum[p, p % NB] = 1.0
    pick = np.tile(np.eye(NB).reshape(-1), (P, 1))
    lower = np.zeros((P, NBLK * NBLK))
    for n in range(NBLK):
        lower[:, n * NBLK:n * NBLK + n] = 1.0
    again = np.tile(np.eye(P, NB), (1, AH))
    again = np.tile(np.eye(P, NB), (1, AH))
    again = np.tile(np.eye(P, NB), (1, AH))
    again = np.tile(np.eye(P, NB), (1, AH))
    again = np.tile(np.eye(P, NB), (1, AH))
    again = np.tile(np.eye(P, NB), (1, AH))
    again = np.tile(np.eye(P, NB), (1, AH))
    again = np.tile(np.eye(P, NB), (1, AH))
    again = np.tile(np.eye(P, NB), (1, AH))
    iota = np.tile(np.arange(PK), (P, 1))
    cst = np.concatenate([eye, upto, past_t, past_s, head_sum, pick, lower, iota, again], 1)

    def bucket(d):
        d = np.maximum(d, 0)
        far = 16 + (np.log(np.maximum(d, 1) / 16.0) / np.log(8.0) * 16).astype(np.int64)
        return np.where(d < 16, d, np.minimum(far, NBUCK - 1))

    dist = 255 - np.arange(RPITCH)
    one = np.zeros((NBUCK + 1, RPITCH + PG))
    one[bucket(dist), np.arange(RPITCH)] = dist >= 0
    one[NBUCK, :RPITCH] = dist < 0
    last = PG - np.arange(PG)
    one[bucket(last), RPITCH + np.arange(PG)] = 1.0
    return cst.astype(np.float32), one.astype(np.float32)


C_EYE, C_UPTO, C_PT, C_PS = 0, 128, 256, 384
C_HS, C_PICK, C_LOW, C_IOTA = 512, 520, 584, 648
C_REP = C_IOTA + PK
C_ALL = C_REP + 64


class Tally:

    def __init__(self):
        self.n, self.var = 0, None

    def add(self, k):
        self.n += k
        return self.at()

    def at(self):
        return self.n if self.var is None else self.var + self.n


class Engine:

    def __init__(self, q, sems, name):
        self.q, self.sems, self.name = q, sems, name
        self.tallies, self.last = {}, None

    def tally(self, key):
        return self.tallies.setdefault(key, Tally())

    def sem(self, name):
        return self.sems(name)

    def op(self, ins, name=None, n=1):
        name = name or self.name + "_steps"
        ins.then_inc(self.sem(name), n)
        self.last = (name, self.tally(("made", name)).add(n))
        return ins

    def sync(self):
        self.q.wait_ge(self.sem(self.last[0]), self.last[1])

    def wait(self, name, n=1):
        self.q.wait_ge(self.sem(name), self.tally(("seen", name)).add(n))

    def hold(self):
        self.q.sem_inc(self.sem(self.name + "_go"), 1)

    @contextmanager
    def loop(self, trips, **per):
        keys = {(k.split("__")[0], k.split("__")[1]): v for k, v in per.items()}
        with self.q.Fori(0, trips) as i:
            start = {k: self.tally(k).n for k in keys}
            others = {k: t.n for k, t in self.tallies.items() if k not in keys}
            for k, v in keys.items():
                self.tally(k).var = i * v
            yield i
            for k, v in keys.items():
                t = self.tally(k)
                assert t.n - start[k] == v, (self.name, k, t.n - start[k], v)
            for k, t in self.tallies.items():
                assert k in keys or others.get(k, 0) == t.n, (self.name, k, "moves in a loop")
        for k, v in keys.items():
            t = self.tally(k)
            t.var, t.n = None, start[k] + trips * v
        if self.last:
            self.last = (self.last[0], self.tally(("made", self.last[0])).at())


def build(nc, A, O):
    ctx = ExitStack()
    with ctx:
        made = {}

        def sems(name):
            if name not in made:
                made[name] = ctx.enter_context(nc.semaphore(name))
            return made[name]

        def sb(name, cols, dt=F32, rows=P):
            return ctx.enter_context(nc.sbuf_tensor(name, [rows, cols], dt))

        def dram(name, shape):
            return nc.dram_tensor(name, shape, F32, kind="Internal").ap()

        ring_t = sb("ring", RING * 4096)
        MOD = sb("mod", 6144)
        X = sb("x", 3 * DM)
        HT = sb("ht", KT * R)
        R1 = sb("r1", 17 * 256 + 3 * DM)
        SN = sb("sn", 2560)
        RA = sb("ra", 6144)
        MIX = sb("mix", 3 * DM)
        LT = sb("lt", NB * PG)
        W2 = sb("w2", 1024)
        cst = sb("cst", C_ALL)
        sm = sb("small", 1200)
        tok = sb("idx", 2 * PK, U32)
        ixu = sb("topi", 5 * PK, U32)
        ptab = sb("ptab", NB * NPG, I32)

        eye = cst[:, C_EYE:C_EYE + P]
        eye8 = cst[0:NB, C_EYE:C_EYE + NB]
        upto = cst[:, C_UPTO:C_UPTO + P]
        ring = ring_t[:].rearrange("p (s n) -> p s n", s=RING)
        Xv = X[:].rearrange("p (t n) -> p t n", t=3)
        HTv = HT[:].rearrange("p (k r) -> p k r", k=KT)
        QKT = R1[:, 0:16 * R].rearrange("p (c r) -> p c r", c=16)
        NAT = R1[:, 16 * R:16 * R + 3 * 2 * N].rearrange("p (t n) -> p t n", t=2)
        H2 = R1[:, 0:3 * DM].rearrange("p (t n) -> p t n", t=3)
        QT = R1[:, 3 * DM:3 * DM + 17 * 256].rearrange("p (i s r) -> p i s r", i=17, s=2)
        MIXv = MIX[:].rearrange("p (t n) -> p t n", t=3)
        LTv = LT[:].rearrange("p (b n) -> p b n", b=NB)
        BT = W2[:, 0:P]
        LK = [W2[:, P * (1 + e):P * (2 + e)] for e in range(2)]
        E2 = [W2[:, P * (3 + e):P * (4 + e)] for e in range(2)]
        PT2 = [W2[:, P * (5 + e):P * (6 + e)] for e in range(2)]
        SELB = [W2[0:NB, 7 * P + NB * e:7 * P + NB * (e + 1)] for e in range(2)]
        SKN, SKT = LT[:, 0:256], LT[:, 256:512]
        TMPS, CAND = LT[:, 512:768], LT[:, 768:1024]
        CAND2, OH, QS = W2[:, 0:256], W2[:, 256:768], W2[:, 768:1024]

        at = [0]

        def small(cols):
            at[0] += cols
            assert at[0] <= 1200
            return sm[:, at[0] - cols:at[0]]

        shT, scT1, silT = small(72), small(72), small(72)
        cwT = small(8 * 30)
        cwv = cwT.rearrange("p (c n) -> p c n", c=8)
        G, bg = small(24), small(8)
        G3 = G.rearrange("p (t n) -> p t n", t=3)
        g_ab, g_lf, g_b, g_a = (small(12) for _ in range(4))
        stats = small(3 * 12)
        mv = small(3 * 2)
        rstd = small(3)
        half = small(1)
        a_mx, a_sum, a_ri = small(8), small(8), small(8)
        cm, mprev, mnew, den, den2 = (small(4) for _ in range(5))
        ex = small(16)
        bc8 = small(8)
        nst = small(4)
        tab = small(8)
        gs, rmx, rs, nbT = small(8), small(8), small(8), small(8)
        nl, m8, pn, ri8 = small(8), small(8), small(8), small(8)
        sM = small(4)
        sE = small(12)
        st12 = small(12)
        wcB = small(32)
        evT = small(32)
        numS = small(32)
        smst = small(12)
        wS = [small(PK) for _ in range(2)]
        wA, wB, wG = small(PK), small(PK), [small(PK) for _ in range(2)]
        v2 = small(2 * PK)
        i2f = small(2 * PK)
        bs = [small(PK) for _ in range(2)]
        nbs = [small(1) for _ in range(2)]
        ebs = [small(PK) for _ in range(2)]
        esum = [small(1) for _ in range(2)]
        er = small(1)
        abf = small(2 * PK)
        selk = small(2 * PK)

        bank = [ctx.enter_context(nc.psum_tensor(f"bank{i}", [P, N], F32)) for i in range(8)]

        LB = (0, 1, 5, 6)

        rel = dram("rel_rows", (AH, P, RPITCH))

        QK = RA[:, 0:2048].rearrange("p (c n) -> p c n", c=8)
        KN = RA[:, 2048:2560].rearrange("p (h n) -> p h n", h=MH)
        CT = RA[:, 2560:3072].rearrange("p (h n) -> p h n", h=MH)
        WT = RA[:, 3072:3584].rearrange("p (h n) -> p h n", h=MH)
        ST = RA[:, 3584:4096].rearrange("p (h n) -> p h n", h=MH)
        WV = RA[:, 4096:4608].rearrange("p (h n) -> p h n", h=MH)
        DG = RA[:, 4608:5120].rearrange("p (h n) -> p h n", h=MH)
        TM = RA[:, 5120:5632].rearrange("p (h n) -> p h n", h=MH)
        ones = RA[:, 5632:5760]
        YS = RA[:, 5760:5824].rearrange("p (c b) -> p c b", c=8)
        YT = RA[:, 5824:5888].rearrange("p (c b) -> p c b", c=8)
        CS = RA[:, 0:4096].rearrange("p (b h k) -> p b h k", b=NB, h=MH)
        KQN = RA[0:NB, 4096:5120]
        EV = RA[0:NB, 5120:5632]
        KQW = W2[0:NB, 0:32]
        NS = SN[0:NB, 0:512]
        BK, BV, BO, BQ = 19, 35, 51, 53
        before_k = [16 * len([n for n in range(BK) if n % RING == s]) for s in range(RING)]

        def slot_count(n):
            if n < BK:
                return 16 * (n // RING + 1)
            return before_k[n % RING] + 2 * 512 + 16 * len([m for m in range(BO, n + 1) if m % RING == n % RING])

        def norm_rows(E, t, src, rows, dst, name=None):
            v = nc.vector
            for e in range(2):
                E.op(v.bn_stats(stats[0:rows, t * 12 + 6 * e:t * 12 + 6 * e + 6], src[:, e * N:(e + 1) * N]))
            E.sync()
            E.op(v.bn_aggr(mv[0:rows, 2 * t:2 * t + 2], stats[0:rows, t * 12:t * 12 + 12].rearrange("p (e n) -> p e n", e=2)))
            E.sync()
            E.op(v.tensor_scalar(mv[0:rows, 2 * t + 1:2 * t + 2], mv[0:rows, 2 * t + 1:2 * t + 2], EPS, None, ALU.add), "var_ready")
            E.wait("rstd_ready")
            E.op(v.tensor_scalar(dst, src, mv[0:rows, 2 * t:2 * t + 1], rstd[0:rows, t:t + 1], ALU.subtract, ALU.mult), name)

        block = ctx.enter_context(nc.Block())

        @block.sync
        def _(q):
            def load(dst, src, name):
                q.dma_start(dst, src).then_inc(sems(name), 16)

            def blk(n):
                return ring[:, n % RING, :]

            def slot_free(n):
                if n >= RING:
                    q.wait_ge(sems("blocks_used"), n - RING + 1)

            def weights(n, w, j):
                slot_free(n)
                load(blk(n).rearrange("p (k n) -> p k n", k=KT), w[:, :, j * N:(j + 1) * N], f"slot{n % RING}")

            load(RA[0:NB, 0:DM], A["c_sample"], "c_in")
            load(RA[NB:NB + 1, 0:DM], A["c_prompt"], "c_in")
            load(cst[:], A["consts"], "consts_in")
            w_ada = A["w_ada"].rearrange("o (k p) n -> (o p) k n", p=P)
            w_in = A["w_in"].rearrange("o (k p) n -> (o p) k n", p=P)
            for n in range(12):
                weights(n, w_ada, n)
                if n == 0:
                    load(MOD[0:9, :], A["b_ada"].partition_broadcast(9), "bada_in")
                    load(Xv[:, 0:2, :], A["x_prompt"].rearrange("o (t p) d -> (o p) t d", p=P), "x_in")
                    load(Xv[0:NB, 2, :], A["x_sample"].rearrange("b o d -> (b o) d"), "x_in")
                if n == 1:
                    cw = RA[:, 1024:2048]
                    load(cw[0:4, :], A["conv_w"].rearrange("o j c -> (o j) c"), "cw_in")
                    load(cw[4:5, :], A["conv_b"], "cw_in")
                    load(cw[5:6, 0:AW], A["beta_attn"], "cw_in")
                    load(cw[5:6, AW:DM], A["beta_mlstm"], "cw_in")
                    load(cw[6:30, :], A["state_conv"].rearrange("o b j c -> (o b j) c"), "cw_in")
                    load(RA[0:NBUCK + 1, 2048:2048 + RPITCH + PG], A["onehot"], "tab_in")
                    load(tab[0:NBUCK, :], A["rel_bias_table"], "tab_in")
                    load(LT[:, 0:64].rearrange("p (k n) -> p k n", k=KT), w_in[:, :, 7 * N:7 * N + 8], "wg_in")
                    load(bg, A["b_gate"].partition_broadcast(P), "bgate_in")
                    load(ptab[0:1, :], A["page_table"].rearrange("b n -> (b n)").unsqueeze(0), "ptab_in")
                    load(smst[0:NB, 0:8], A["rel_bias_table"][0:1, :].partition_broadcast(NB), "smst_in")
                    load(smst[0:NB, 8:12], A["state_m"].rearrange("o b h -> (o b) h"), "smst_in")
            for j in range(7):
                weights(12 + j, w_in, j)

            q.wait_ge(sems("rel_ready"), 1)
            q.dma_start(rel, RA[0:AH, 4096:4096 + RPITCH].unsqueeze(1).broadcast_to([AH, P, RPITCH])).then_inc(sems("rel_out"), 16)
            q.wait_ge(sems("rel_out"), 16)
            skew = bass.AP(rel.tensor, P - 1, [[RPITCH - 1, P], [P * RPITCH, AH], [1, 2 * P]])
            q.wait_ge(sems("cwT_ready"), 1)
            load(RA[:, 0:2048].rearrange("p (h n) -> p h n", h=AH), skew, "rel_in")

            q.wait_ge(sems("ptab_in"), 16)
            for pool, base in ((A["cache_k"], BK), (A["cache_v"], BV)):
                pages = pool.rearrange("o g r h d -> (o g) r (h d)")
                with q.Fori(0, 4) as i:
                    for j in range(4):
                        q.wait_ge(sems("blocks_used"), i * 4 + (base + j - RING + 1))
                        for g in range(8):
                            page = q.value_load(ptab[0:1, bass.ds(i * 32 + (j * 8 + g), 1)], min_val=0, max_val=159)
                            q.dma_start(blk(base + j)[:, g * N:(g + 1) * N],
                                        pages[bass.ds(page, 1), :, :].rearrange("g r n -> (g r) n")
                                        ).then_inc(sems(f"slot{(base + j) % RING}"), 16)
            w_o = A["w_out"].rearrange("o (k p) n -> (o p) k n", p=P)
            w_q = A["w_query"].rearrange("o (k p) n -> (o p) k n", p=P)
            for j in range(2):
                weights(BO + j, w_o, j)
            for j in range(2):
                weights(BQ + j, w_q, j)
            q.wait_ge(sems("satt_done"), 1)
            load(CS.rearrange("p b h k -> p (b h) k"), A["state_C"].rearrange("o b h v k -> v (o b h) k"), "cs_in")
            load(NS.rearrange("b (h k) -> b h k", h=MH), A["state_n"].rearrange("o b h k -> (o b) h k"), "ns_in")
            load(SKN.rearrange("p (s d) -> p s d", s=2), A["sub_keys"].rearrange("o s n d -> (o n) s d"), "sk_in")
            q.wait_ge(sems("cs_stored"), 16)
            load(RA[:, 0:DM], A["ln1_g"].partition_broadcast(P), "ln1_in")
            load(RA[:, DM:2 * DM], A["ln1_b"].partition_broadcast(P), "ln1_in")
            for j in range(2, 4):
                weights(BQ + j, w_q, j)
            q.wait_ge(sems("h2_ready"), 3)
            load(RA[:, 0:DM], A["ln2_g"].partition_broadcast(P), "ln2_in")
            load(RA[:, DM:2 * DM], A["ln2_b"].partition_broadcast(P), "ln2_in")

        @block.gpsimd
        def _(q):
            E = Engine(q, sems, "pool")
            g = nc.gpsimd
            E.op(g.memset(half[:], -0.5))
            E.sync()

            def rsqrt(t):
                rows = P if t < 2 else NB
                E.wait("var_ready")
                E.op(g.tensor_tensor(rstd[0:rows, t:t + 1], mv[0:rows, 2 * t + 1:2 * t + 2], half[0:rows, :], ALU.pow), "rstd_ready")

            for t in range(3):
                rsqrt(t)
            for t in range(3):
                rsqrt(t)
                rsqrt(t)

            eu = A["expert_u"].rearrange("o e d -> (o e) d")
            ev = A["expert_v"].rearrange("o e d -> (o e) d")

            def head(par, rows):
                E.wait("idx_ready")
                E.hold()
                for name, table, off in (("u", eu, 0), ("v", ev, UR * DM)):
                    for k in range(PK):
                        E.wait(name + "_slot_free")
                        E.hold()
                        s = k % UR
                        g.indirect_dma_start(ring_t[0:rows, off + s * DM:off + (s + 1) * DM], None, table,
                                             bass.IndirectOffsetOnAxis(tok[0:rows, par * PK + k:par * PK + k + 1], 0)
                                             ).then_inc(sems(f"{name}{s}_in"), 16)

            E.wait("queries_done")
            E.hold()
            for t in range(NT):
                with E.loop(PH // 2, seen__idx_ready=2, seen__u_slot_free=2 * PK, seen__v_slot_free=2 * PK):
                    head(0, P)
                    head(1, P)
            head(0, AH * NB)
            for t in range(3):
                rsqrt(t)

        @block.tensor
        def _(q):
            E = Engine(q, sems, "pe")

            def mm(out, lhsT, rhs, start=True, stop=True):
                return nc.tensor.matmul(out, lhsT, rhs, start=start, stop=stop)

            def acc(out, lhsT, rhs):
                return nc.tensor.matmul(out, lhsT, rhs, start=False, stop=False, skip_group_check=True)

            def zero(out, rows, zeros):
                return nc.tensor.matmul(out, zeros[:, 0:rows], zeros, start=True, stop=False, skip_group_check=True)

            def tr(out, in_):
                rows = in_.shape[0]
                return nc.tensor.transpose(out, in_, cst[0:rows, C_EYE:C_EYE + rows])

            def block_in(n):
                q.wait_ge(sems(f"slot{n % RING}"), slot_count(n))

            def used():
                E.sync()
                q.sem_inc(sems("blocks_used"), 1)

            q.wait_ge(sems("consts_in"), 16)
            E.wait("setup_in")
            for k in range(KT):
                m = tr(bank[7][:, 9 * k:9 * k + 9], MIXv[0:9, 0, k * P:(k + 1) * P])
            E.op(m, "setup_mm")
            E.wait("setup_in")
            for n in range(12):
                block_in(n)
                if n >= 2:
                    E.wait("ada_out")
                for k in range(KT):
                    m = mm(bank[n % 2][0:9, :], silT[:, 9 * k:9 * k + 9], ring[:, n % RING, k * N:(k + 1) * N],
                           start=(k == 0), stop=(k == KT - 1))
                E.op(m, "ada_mm")
                used()
            E.wait("ada_out", 2)
            for k in range(16):
                m = tr(bank[7][:, 9 * k:9 * k + 9], MOD[0:9, k * P:(k + 1) * P])
            E.op(m, "setup_mm")
            q.wait_ge(sems("cw_in"), 80)
            for k in range(KT):
                m = tr(bank[6][:, 30 * k:30 * k + 30], RA[0:30, 1024 + k * P:1024 + (k + 1) * P])
            E.op(m, "setup_mm")
            q.wait_ge(sems("tab_in"), 32)
            E.op(mm(bank[5][0:AH, 0:RPITCH], tab[0:NBUCK + 1, :], RA[0:NBUCK + 1, 2048:2048 + RPITCH]), "setup_mm")
            E.wait("setup_in")
            mm(bank[4][:, 0:P], RA[0:NBUCK, 2560:2688], RA[0:NBUCK, 2048 + RPITCH:2048 + RPITCH + PG], stop=False)
            E.op(mm(bank[4][:, 0:P], RA[0:NBUCK, 2688:2816],
                    cst[0:NBUCK, NBUCK - 1:NBUCK].broadcast_to([NBUCK, P]), start=False), "setup_mm")

            for t in range(3):
                rows = P if t < 2 else NB
                E.wait("xhat_ready")
                if t >= 1:
                    E.wait("xT_out")
                for k in range(KT):
                    m = tr(bank[k // 4][:, (k % 4) * rows:(k % 4 + 1) * rows], H2[0:rows, t, k * P:(k + 1) * P])
                E.op(m, "xT")
            E.wait("xT_out")

            job = [0]

            def proj_bank():
                job[0] += 1
                if job[0] > 4:
                    E.wait("proj_out")
                return bank[(job[0] - 1) % 4]

            for j in range(7):
                n = 12 + j
                block_in(n)
                if j in (0, 1, 3, 4):
                    for c in range(4):
                        b = proj_bank()
                        for k in range(KT):
                            m = mm(b[:, 0:R], ring[:, n % RING, k * N + c * P:k * N + (c + 1) * P], HTv[:, k, :],
                                   start=(k == 0), stop=(k == KT - 1))
                        E.op(m, "proj_mm")
                else:
                    for t in range(3):
                        b = proj_bank()
                        r0, rows = t * P, (P if t < 2 else NB)
                        for k in range(KT):
                            m = mm(b[0:rows, :], HTv[:, k, r0:r0 + rows], ring[:, n % RING, k * N:(k + 1) * N],
                                   start=(k == 0), stop=(k == KT - 1))
                        E.op(m, "proj_mm")
                used()
            q.wait_ge(sems("wg_in"), 16)
            for t in range(3):
                b = proj_bank()
                r0, rows = t * P, (P if t < 2 else NB)
                for k in range(KT):
                    m = mm(b[0:rows, 0:8], HTv[:, k, r0:r0 + rows], LT[:, k * 8:(k + 1) * 8], start=(k == 0), stop=(k == KT - 1))
                E.op(m, "proj_mm")
            E.wait("proj_out", 4)

            for t in range(2):
                for c in range(4):
                    m = tr(bank[t][:, c * P:(c + 1) * P], QKT[:, 4 + c, t * P:(t + 1) * P])
                E.op(m, "nat_T")
            for c in range(8):
                m = tr(bank[2 + c // 4][0:NB, (c % 4) * P:(c % 4 + 1) * P], QKT[:, c, SEQ:R])
            E.op(m, "nat_T")
            for c in range(8):
                m = tr(bank[5 + c // 4][0:11, (c % 4) * P:(c % 4 + 1) * P], QKT[:, 8 + c, SEQ - 3:R])
            E.op(m, "nat_T")
            E.wait("nat_out", 4)

            L = RA[:, 2048:4096].rearrange("p (h n) -> p h n", h=AH)
            PT = RA[:, 4096:6144].rearrange("p (h n) -> p h n", h=AH)
            for t in range(NT):
                w = P * (t + 1)
                for h2 in range(4):
                    if h2 + 4 * t >= 2:
                        E.wait("logits_used")
                    for e in range(2):
                        hp = slice(64 * e, 64 * e + 64)
                        m = mm(bank[LB[2 * (h2 % 2) + e]][:, 0:w], QKT[hp, h2, t * P:(t + 1) * P], QKT[hp, 4 + h2, 0:w])
                    E.op(m, "logits")
                E.wait("probs")
                for s in range(t + 1):
                    for hh in range(2):
                        if (t, s, hh) != (0, 0, 0):
                            E.wait("probsT_out")
                        for e in range(4):
                            m = tr(bank[2][:, e * P:(e + 1) * P], L[:, 4 * hh + e, s * P:(s + 1) * P])
                        E.op(m, "probsT")
                E.wait("probsT_out")
                for h in range(AH):
                    for s in range(t + 1):
                        m = mm(bank[3 + t][:, h * AD:(h + 1) * AD], PT[:, h, s * P:(s + 1) * P],
                               NAT[:, s, h * AD:(h + 1) * AD], start=(s == 0), stop=(s == t))
                E.op(m, "attn_mm")
                if t == 0:
                    E.tally(("seen", "probsT_out")).n -= 1
            E.wait("logits_used", 2)
            E.wait("attn_out", 2)

            E.wait("logf_ready")
            E.op(mm(bank[0][:, 0:12], upto, g_lf), "cum")
            E.wait("conv_ready")
            for c in range(2):
                cs = slice(c * P, (c + 1) * P)
                for h in range(MH):
                    m = tr(bank[1][:, h * P:(h + 1) * P], QK[:, MH + h, cs])
                E.op(m, "kn_T")
                for h in range(MH):
                    m = mm(bank[2][:, h * P:(h + 1) * P], QK[:, MH + h, cs], QK[:, h, cs])
                E.op(m, "kq")
                E.wait("diag_a")
                E.op(mm(bank[3][:], ones, RA[:, 4608:5120]), "a_rows")
                E.wait("mm_diag")
                E.op(mm(bank[4][:], ones, RA[:, 4608:5120]), "m_rows")
                E.op(mm(bank[0][:, 16:24], cst[:, C_EYE + P - 1:C_EYE + P].broadcast_to([P, P]), bc8), "last_row")
                if c == 1:
                    for h in range(MH):
                        mm(bank[5][:, h * P:(h + 1) * P], QK[:, h, cs], CT[:, h, :])
                    for h in range(MH):
                        m = mm(bank[3][:, h:h + 1], QK[:, h, cs], nst[:, h:h + 1])
                    E.op(m, "inter")
                E.wait("st_ready")
                for h in range(MH):
                    mm(bank[6][:, h * P:(h + 1) * P], ST[:, h, :], NAT[:, c, N + h * P:N + (h + 1) * P])
                for h in range(MH):
                    m = mm(bank[4][:, h:h + 1], ST[:, h, :], ones[:, 0:1])
                E.op(m, "intra")
                E.wait("wv_ready")
                E.wait("kn_out")
                for h in range(MH):
                    mm(bank[7][:, h * P:(h + 1) * P], KN[:, h, :], WV[:, h, :])
                for h in range(MH):
                    m = mm(bank[2][:, h:h + 1], KN[:, h, :], ex[:, 8 + h:9 + h])
                E.op(m, "state_mm")
                E.wait("chunk_done")
            for h in range(MH):
                tr(bank[1][:, h * P:(h + 1) * P], CT[:, h, :])
            E.op(tr(bank[2][0:MH, 0:P], nst), "state_T")
            E.wait("state_T_out")

            E.wait("qd_ready")
            QD = RA[0:NB, 0:9 * N]
            E.wait("q_rows_used")
            E.op(mm(bank[0][:], ones[0:NB, :], QD[:, 0:N]), "q_rows")
            q.sem_inc(sems("lt_T"), 2)
            E.tally(("made", "lt_T")).n = 2
            with E.loop(4, made__q_rows=2, seen__q_rows_used=2, seen__k_logits=2, seen__lt_out=2, made__lt_T=2) as i:
                for e in range(2):
                    E.wait("q_rows_used")
                    E.op(mm(bank[1 - e][:], ones[0:NB, :], QD[:, bass.ds(i * (2 * N) + (e + 1) * N, N)]), "q_rows")
                    E.wait("k_logits")
                    E.wait("lt_out")
                    E.op(tr(bank[2 + e][:, 0:P], LK[e]), "lt_T")
            E.wait("lt_out", 2)
            E.wait("gate_in")
            tr(bank[4][0:NB, 0:P], gs)
            E.op(tr(bank[4][0:NB, P:2 * P], rmx), "gate_mm")
            E.wait("gate_in")
            E.op(tr(bank[4][:, 256:256 + NB], RA[0:NB, 5000:5128]), "gate_mm")
            E.wait("nbT_ready")
            zero(bank[6][0:NB, :], NB, RA[0:NB, 8 * N:9 * N])
            E.tally(("made", "blocks_used")).n = BV
            with E.loop(4, made__v_mm=2, seen__exp_b=2, made__pT=2, seen__pT_out=2, seen__diag_v=2, made__v_sum=2,
                        made__v_half=2) as i:
                for e in range(2):
                    E.wait("exp_b")
                    E.op(tr(bank[2 + e][:, 0:P], E2[e]), "pT")
                    E.wait("pT_out")
                    for hf in range(2):
                        n = BV + e * 2 + hf
                        q.wait_ge(sems(f"slot{n % RING}"), i * 128 + (before_k[n % RING] + 512 + 128))
                        for g in range(8):
                            pg = hf * 8 + g
                            m = mm(bank[4 + e][0:AH, :], PT2[e][:, pg * 8:pg * 8 + 8], ring[:, n % RING, g * N:(g + 1) * N],
                                   start=(pg == 0), stop=(pg == 15))
                        E.op(m, "v_mm" if hf else "v_half")
                        used()
                    E.wait("diag_v")
                    E.hold()
                    E.op(acc(bank[6][0:NB, :], SELB[e], RA[0:NB, e * N:(e + 1) * N]), "v_sum")
            E.wait("exps_done")
            E.op(tr(bank[7][0:NB, 0:P], rs), "gate_mm")

            for c in range(8):
                m = tr(bank[c // 4][0:NB, (c % 4) * P:(c % 4 + 1) * P], YS[:, (c + 4) % 8, :])
            E.op(m, "kqn_T")
            E.wait("smem_in")
            E.op(mm(bank[2][:, 0:32], ones[0:NB, :], KQW), "smem_mm")
            E.wait("smem_in")
            for h in range(MH):
                m = tr(bank[3][:, h * 8:(h + 1) * 8], EV[:, h * P:(h + 1) * P])
            E.op(m, "smem_mm")
            E.wait("kqn_out")
            E.wait("ev_out")
            for b in range(NB):
                if b >= 2:
                    E.wait("kq_used")
                one = cst[0:NB, C_EYE + b:C_EYE + b + 1].broadcast_to([NB, P])
                mm(bank[b % 2][:], one, KQN[:, 0:N])
                E.op(mm(bank[4 + b % 2][:], one, KQN[:, N:2 * N]), "kq_rows")
            E.wait("c_new")
            for h in range(MH):
                m = tr(bank[3][0:NB, h * P:(h + 1) * P], numS[:, h * 8:(h + 1) * 8])
            E.op(m, "smem_mm")
            E.wait("smem_done")

            for t in range(3):
                r0, rows = t * P, (P if t < 2 else NB)
                for k in range(KT):
                    m = tr(bank[k // 4][:, (k % 4) * rows:(k % 4 + 1) * rows], MIXv[0:rows, t, k * P:(k + 1) * P])
                E.op(m, "tail_mm")
                E.wait("mixT_out")
            E.wait("cs_gone")
            one = cst[0:9, C_EYE + 8:C_EYE + 9].broadcast_to([9, P])
            for v, col in enumerate((2 * DM, 4 * DM, 3 * DM)):
                if v:
                    E.wait("bc_out")
                for e in range(2):
                    m = mm(bank[6 + e][:], one, MOD[0:9, col + e * N:col + (e + 1) * N])
                E.op(m, "tail_mm")
            for j in range(2):
                n = BO + j
                block_in(n)
                for t in range(3):
                    r0, rows = t * P, (P if t < 2 else NB)
                    for k in range(KT):
                        m = mm(bank[3 * j + t][0:rows, :], HTv[:, k, r0:r0 + rows], ring[:, n % RING, k * N:(k + 1) * N],
                               start=(k == 0), stop=(k == KT - 1))
                E.op(m, "y_mm")
                used()
            E.wait("bc_out")
            for t in range(3):
                rows = P if t < 2 else NB
                E.wait("h2_ready")
                for k in range(KT):
                    m = tr(bank[6 + k // 4][:, (k % 4) * rows:(k % 4 + 1) * rows], H2[0:rows, t, k * P:(k + 1) * P])
                E.op(m, "tail_mm")
                E.wait("h2T_out")
            for e in range(2):
                m = mm(bank[6 + e][0:64, :], cst[0:NB, C_REP:C_REP + 64], H2[0:NB, 2, e * N:(e + 1) * N])
            E.op(m, "tail_mm")
            q.wait_ge(sems("sk_in"), 16)
            for e in range(2):
                m = tr(bank[5][:, e * P:(e + 1) * P], SKN[:, e * P:(e + 1) * P])
            E.op(m, "tail_mm")
            for c in range(16):
                n = BQ + c // 4
                if c % 4 == 0:
                    block_in(n)
                if c >= 4:
                    E.wait("q_out")
                for k in range(KT):
                    m = mm(bank[c % 4][:, 0:R], ring[:, n % RING, k * N + (c % 4) * P:k * N + (c % 4 + 1) * P], HTv[:, k, :],
                           start=(k == 0), stop=(k == KT - 1))
                E.op(m, "tail_mm")
                if c % 4 == 3:
                    used()
            E.wait("q_out", 4)
            E.wait("h2r_out")
            for e in range(2):
                m = mm(bank[6 + e][:], one, MOD[0:9, 5 * DM + e * N:5 * DM + (e + 1) * N])
            E.op(m, "tail_mm")
            E.wait("g2_out")
            E.wait("sk_out")

            E.wait("zeros_ready")
            q.sem_inc(sems("v_slot_free"), UR)
            E.tally(("made", "v_slot_free")).n = UR
            E.tally(("seen", "diag_w")).n = 2 * PK
            E.tally(("made", "scores")).n = 1

            def scores():
                E.wait("qs_ready")
                E.wait("scores_used")
                for e in range(2):
                    m = mm(bank[0][:, e * P:(e + 1) * P], QS[:, e * P:(e + 1) * P], SKT[:, e * P:(e + 1) * P])
                E.op(m, "scores")

            vcount = [0] * UR

            def head(par, rows, fb, base, i=None):
                out_rows = P if rows == P else NB
                for k in range(PK):
                    s = k % UR
                    count = 16 * (base + par * 2 + k // UR + 1)
                    q.wait_ge(sems(f"v{s}_in"), count if i is None else i * 64 + count)
                    E.wait("diag_w")
                    for e in range(2):
                        m = acc(bank[fb + e][0:out_rows, :], MIX[0:rows, (k % 4) * P:(k % 4) * P + out_rows],
                                ring_t[0:rows, (UR + s) * DM + e * N:(UR + s) * DM + (e + 1) * N])
                    E.op(m, "v_slot_free")

            scores()
            for t in range(NT):
                fb = 4 + 2 * t
                zero(bank[fb][:], P, MIX[0:NB, 2048:2560])
                zero(bank[fb + 1][:], P, MIX[0:NB, 2048:2560])
                with E.loop(PH // 2, seen__qs_ready=2, seen__scores_used=2, made__scores=2, seen__diag_w=2 * PK,
                            made__v_slot_free=2 * PK) as i:
                    for par in range(2):
                        scores()
                        head(par, P, fb, t * 2 * PH, i)
                E.sync()
                q.sem_inc(sems("f_ready"), 1)
            zero(bank[2][0:NB, :], NB, MIX[0:NB, 2048:2560])
            zero(bank[3][0:NB, :], NB, MIX[0:NB, 2048:2560])
            head(0, AH * NB, 2, 4 * PH)
            E.sync()
            q.sem_inc(sems("f_ready"), 1)

        @block.scalar
        def _(q):
            E = Engine(q, sems, "act")
            a = nc.scalar
            stores = [0]

            def store(dst, src, name="stored"):
                q.dma_start(dst, src).then_inc(sems(name), 16)
                stores[0] += 16 * (name == "stored")

            q.wait_ge(sems("c_in"), 32)
            E.op(a.activation(MIX[0:9, 1024:2048], RA[0:9, 0:DM], ACT.Exp, scale=-1.0), "pre_exp")
            E.wait("mods_T")
            for t in range(2):
                E.wait("xT")
                for k in range(KT):
                    m = a.activation(HTv[:, k, t * P:(t + 1) * P], bank[k // 4][:, (k % 4) * P:(k % 4 + 1) * P],
                                     ACT.Identity, scale=scT1[:, 9 * k + 8:9 * k + 9], bias=shT[:, 9 * k + 8:9 * k + 9])
                E.op(m, "xT_out")
            job = [0]

            def out(dst, rows, cols):
                E.wait("proj_mm")
                E.op(a.activation(dst, bank[job[0] % 4][0:rows, 0:cols], ACT.Copy), "proj_out")
                job[0] += 1

            for j, dst in enumerate((0, 4, None, 8, 12, None, None)):
                if dst is not None:
                    for c in range(4):
                        out(QKT[:, dst + c, :], P, R)
                else:
                    o = {2: 0, 5: 1, 6: 2}[j]
                    for t in range(2):
                        out(NAT[:, t, o * N:(o + 1) * N], P, N)
                    out(SN[0:NB, 1024 + o * N:1024 + (o + 1) * N], NB, N)
            E.wait("g_zero")
            for t in range(3):
                out(G3[0:P if t < 2 else NB, t, :], P if t < 2 else NB, 8)
            for t in range(2):
                E.wait("nat_T")
                E.op(a.activation(MIX[:, t * N:(t + 1) * N], bank[t][:], ACT.Copy), "nat_out")
            E.wait("nat_T")
            E.op(a.activation(SN[0:NB, 0:N], bank[2][0:NB, :], ACT.Copy))
            E.op(a.activation(SN[0:NB, N:2 * N], bank[3][0:NB, :], ACT.Copy), "nat_out")
            E.wait("nat_T")
            E.op(a.activation(MIX[0:11, 1024:1536], bank[5][0:11, :], ACT.Copy))
            E.op(a.activation(MIX[0:11, 1536:2048], bank[6][0:11, :], ACT.Copy), "nat_out")
            E.sync()
            kp, vp = (O[n].rearrange("o b s h d -> (o b s) (h d)") for n in ("k_prompt", "v_prompt"))
            ks, vs = (O[n].rearrange("o b s h d -> (o b s) (h d)") for n in ("k_sample", "v_sample"))
            store(kp.rearrange("(t p) n -> p t n", p=P), MIX[:, 0:1024].rearrange("p (t n) -> p t n", t=2))
            store(vp.rearrange("(t p) n -> p t n", p=P), NAT[:, :, 0:N])
            store(ks, SN[0:NB, N:2 * N])
            store(vs, SN[0:NB, 2 * N:3 * N])
            store(O["conv_prompt"].rearrange("o b j c -> (o b j) c"), MIX[0:3, 1024:2048])
            store(O["conv_sample"].rearrange("o b j c -> (o b) j c")[:, 2, :], MIX[3:11, 1024:2048])
            store(O["conv_sample"].rearrange("o b j c -> (o b) j c")[:, 0:2, :],
                  A["state_conv"].rearrange("o b j c -> (o b) j c")[:, 1:3, :])
            q.wait_ge(sems("stored"), stores[0])
            q.sem_inc(sems("rows_stored"), 1)
            L = RA[:, 2048:4096].rearrange("p (h n) -> p h n", h=AH)
            for t in range(NT):
                E.wait("row_max")
                for h in range(AH):
                    m = a.activation(L[:, h, 0:P * (t + 1)], L[:, h, 0:P * (t + 1)], ACT.Exp, bias=a_mx[:, h:h + 1],
                                     accum_out=a_sum[:, h:h + 1])
                E.op(m, "probs")
            E.wait("pre_arg")
            E.op(a.activation(g_ab, g_ab, ACT.Exp, scale=-1.0))
            E.sync()
            E.op(a.activation(g_ab, g_ab, ACT.Ln, bias=1.0), "pre_exp")
            E.wait("pre_arg")
            E.op(a.activation(RA[:, 2048:4096], RA[:, 0:2048], ACT.Exp, scale=-1.0))
            E.op(a.activation(RA[:, 5824:5888], RA[:, 5760:5824], ACT.Exp, scale=-1.0), "pre_exp")
            E.op(a.activation(MIXv[:, 0:2, N:2 * N], NAT[:, :, 2 * N:3 * N], ACT.Exp, scale=-1.0))
            E.op(a.activation(MIX[0:NB, 2560:3072], SN[0:NB, 2048:2560], ACT.Exp, scale=-1.0), "pre_exp")
            for c in range(2):
                E.wait("kn_T")
                if c == 0:
                    E.wait("conv_ready")
                E.op(a.activation(RA[:, 2048:2560], bank[1][:], ACT.Copy), "kn_out")
                E.wait("ex_args")
                E.op(a.activation(ex, ex, ACT.Exp), "ex_ready")
                for h in range(MH):
                    m = a.activation(WT[:, h, :], WT[:, h, :], ACT.Exp, bias=g_a[:, 4 * c + h:4 * c + h + 1])
                E.op(m, "wt_ready")
            E.wait("state_T")
            E.op(a.activation(RA[:, 4096:4608], bank[1][:], ACT.Copy))
            E.op(a.activation(RA[0:MH, 4608:4736], bank[2][0:MH, 0:P], ACT.Copy), "state_T_out")
            E.sync()
            store(O["C_prompt"].rearrange("o b h v k -> v (o b h) k"), WV)
            store(O["n_prompt"].rearrange("o b h k -> (o b h) k"), RA[0:MH, 4608:4736])
            store(O["m_prompt"].rearrange("o b h -> (o b) h"), mprev[0:1, :])
            q.wait_ge(sems("stored"), stores[0])
            q.sem_inc(sems("state_stored"), 1)
            q.sem_inc(sems("lt_out"), 2)
            E.tally(("made", "lt_out")).n = 2
            E.tally(("seen", "lt_T")).n = 2
            with E.loop(4, seen__lt_T=2, made__lt_out=2) as i:
                for e in range(2):
                    E.wait("lt_T")
                    E.op(a.activation(LT[:, bass.ds(i * 256 + e * P, P)], bank[2 + e][:, 0:P], ACT.Copy, scale=SC_A,
                                      accum_out=gs[:, bass.ds(i * 2 + e, 1)]), "lt_out")
            E.wait("nbT_ready")
            E.op(a.activation(pn[0:NB, :], pn[0:NB, :], ACT.Exp), "pn_ready")
            with E.loop(4, made__exp_b=2, seen__pT=2, made__pT_out=2) as i:
                for e in range(2):
                    E.op(a.activation(E2[e], LT[:, bass.ds(i * 256 + e * P, P)], ACT.Exp,
                                      bias=nbT[:, bass.ds(i * 2 + e, 1)], accum_out=rs[:, bass.ds(i * 2 + e, 1)]), "exp_b")
                for e in range(2):
                    E.wait("pT")
                    E.op(a.activation(PT2[e], bank[2 + e][:, 0:P], ACT.Copy), "pT_out")
            E.sync()
            q.sem_inc(sems("exps_done"), 1)
            E.wait("kqn_T")
            E.wait("satt_done")
            E.op(a.activation(KQN[:, 0:N], bank[0][0:NB, :], ACT.Copy))
            E.op(a.activation(KQN[:, N:2 * N], bank[1][0:NB, :], ACT.Copy), "kqn_out")
            E.wait("sE_args")
            E.op(a.activation(sE[0:NB, :], sE[0:NB, :], ACT.Exp), "sE_ready")
            E.wait("c_new")
            store(O["C_sample"].rearrange("o b h v k -> v (o b h) k"), CS.rearrange("p b h k -> p (b h) k"), "cs_stored")
            store(O["n_sample"].rearrange("o b h k -> (o b) h k"), NS.rearrange("b (h k) -> b h k", h=MH))
            store(O["m_sample"].rearrange("o b h -> (o b) h"), sM[0:NB, :])
            for t in range(3):
                r0, rows = t * P, (P if t < 2 else NB)
                E.wait("tail_mm")
                for k in range(KT):
                    m = a.activation(HTv[:, k, r0:r0 + rows], bank[k // 4][:, (k % 4) * rows:(k % 4 + 1) * rows],
                                     ACT.Copy, scale=cwT[:, 30 * k + 5:30 * k + 6])
                E.op(m, "mixT_out")
            q.wait_ge(sems("cs_stored"), 16)
            q.sem_inc(sems("cs_gone"), 1)
            for v in range(3):
                E.wait("tail_mm")
                for e in range(2):
                    m = a.activation(RA[:, 2048 + v * DM + e * N:2048 + v * DM + (e + 1) * N], bank[6 + e][:], ACT.Copy)
                    if e == 0:
                        E.op(m)
                E.op(m, "bc_out")
            for t in range(3):
                r0, rows = t * P, (P if t < 2 else NB)
                E.wait("tail_mm")
                for e in range(2):
                    m = a.activation(HTv[:, 4 * e:4 * e + 4, r0:r0 + rows],
                                     bank[6 + e][:, 0:4 * rows].rearrange("p (k r) -> p k r", k=4), ACT.Copy)
                    if e == 0:
                        E.op(m)
                E.op(m, "h2T_out")
            E.wait("tail_mm")
            for e in range(2):
                m = E.op(a.activation(RA[0:64, 5120 + e * N:5120 + (e + 1) * N], bank[6 + e][0:64, :], ACT.Copy),
                         "h2r_out" if e else None)
            E.wait("tail_mm")
            E.op(a.activation(SKT, bank[5][:, 0:256], ACT.Copy), "sk_out")
            E.wait("qt_zero")
            for c in range(16):
                E.wait("tail_mm")
                h, e = c // 2, c % 2
                E.op(a.activation(QT[:, h:h + PH + 1:PH, e, :], bank[c % 4][:, 0:SEQ].rearrange("p (t r) -> p t r", t=2), ACT.Copy))
                E.op(a.activation(QT[:, 16, e, h * NB:(h + 1) * NB], bank[c % 4][:, SEQ:R], ACT.Copy), "q_out")
            E.sync()
            q.sem_inc(sems("queries_done"), 1)
            E.wait("tail_mm")
            q.wait_ge(sems("stored"), stores[0])
            for e in range(2):
                m = E.op(a.activation(RA[:, 2048 + e * N:2048 + (e + 1) * N], bank[6 + e][:], ACT.Copy), "g2_out" if e else None)

            E.tally(("seen", "v_slot_free")).n = UR - 4
            E.tally(("made", "diag_w")).n = 2 * PK

            QTf = R1[:, 3 * DM:3 * DM + 17 * 256]

            def next_query(off):
                E.wait("scores")
                E.op(a.activation(QS, QTf[:, off], ACT.Copy), "qs_ready")

            def head(par, rows, nxt=None):
                if nxt is not None:
                    next_query(nxt)
                E.wait("gelu_arg")
                E.op(a.activation(wB[0:rows, :], wB[0:rows, :], ACT.Exp), "gelu_exp")
                E.wait("w_ready")
                out_rows = P if rows == P else NB
                src = eye if rows == P else cst[0:rows, C_HS:C_HS + NB]
                for k in range(PK):
                    E.wait("v_slot_free")
                    E.op(a.activation(MIX[0:rows, (k % 4) * P:(k % 4) * P + out_rows], src, ACT.Copy,
                                      scale=wG[par][0:rows, k:k + 1]), "diag_w")
                if nxt is not None:
                    best(1 - par)

            def best(par):
                E.wait("best_ready")
                E.op(a.activation(ebs[par], bs[par], ACT.Exp, bias=nbs[par], accum_out=esum[par]), "best_exp")

            q.sem_inc(sems("scores"), 1)
            next_query(slice(0, 256))
            best(0)
            for t in range(NT):
                with E.loop(PH // 2, seen__scores=2, made__qs_ready=2, seen__gelu_arg=2, made__gelu_exp=2, seen__w_ready=2,
                            seen__v_slot_free=2 * PK, made__diag_w=2 * PK, seen__best_ready=2, made__best_exp=2) as i:
                    for par in range(2):
                        head(par, P, bass.ds(i * 512 + (t * PH + par + 1) * 256, 256))
            head(0, AH * NB)
            for t in range(3):
                E.wait("y_ready")
                if t < 2:
                    store(O["y_prompt"].rearrange("o (t p) d -> (o p) t d", p=P)[:, t, :], Xv[:, t, :])
                else:
                    store(O["y_sample"].rearrange("b o d -> (b o) d"), Xv[0:NB, 2, :])
            q.wait_ge(sems("stored"), stores[0])

        @block.vector
        def _(q):
            E = Engine(q, sems, "dve")
            v = nc.vector

            def step(ins, name=None):
                E.op(ins, name)
                E.sync()

            E.op(v.memset(G, 0.0), "g_zero")
            E.op(v.memset(tab[NBUCK:NBUCK + 1, :], NEG))
            E.wait("pre_exp")
            silu = MIX[0:9, 0:DM]
            e_ = MIX[0:9, 1024:2048]
            step(v.tensor_scalar(e_, e_, 1.0, None, ALU.add))
            step(v.reciprocal(e_, e_))
            E.op(v.tensor_tensor(silu, e_, RA[0:9, 0:DM], ALU.mult), "setup_in")
            E.wait("setup_mm")
            E.op(v.tensor_copy(silT, bank[7][:, 0:72]), "setup_in")
            q.wait_ge(sems("tab_in"), 32)
            step(v.memset(RA[0:NBUCK, 2560:2816], 0.0))
            E.op(v.tensor_copy(RA[0:NBUCK, 2560 + 120:2688], tab[0:NBUCK, :]))
            E.op(v.tensor_copy(RA[0:NBUCK, 2688:2808].rearrange("p (g h) -> p g h", g=15),
                               tab[0:NBUCK, :].unsqueeze(1).broadcast_to([NBUCK, 15, AH])), "setup_in")
            q.wait_ge(sems("x_in"), 32)
            for t in range(3):
                rows = P if t < 2 else NB
                norm_rows(E, t, Xv[0:rows, t, :], rows, H2[0:rows, t, :], "xhat_ready")
            q.wait_ge(sems("bada_in"), 16)
            for n in range(12):
                E.wait("ada_mm")
                E.op(v.tensor_tensor(MOD[0:9, n * N:(n + 1) * N], bank[n % 2][0:9, :], MOD[0:9, n * N:(n + 1) * N], ALU.add), "ada_out")
            E.wait("setup_mm")
            E.op(v.tensor_copy(shT, bank[7][:, 0:72]))
            E.op(v.tensor_scalar(scT1, bank[7][:, 72:144], 1.0, None, ALU.add), "mods_T")
            E.wait("setup_mm")
            E.op(v.tensor_copy(cwT, bank[6][:, 0:240]), "cwT_ready")
            E.wait("setup_mm")
            E.op(v.tensor_copy(RA[0:AH, 4096:4096 + RPITCH], bank[5][0:AH, 0:RPITCH]), "rel_ready")
            E.wait("setup_mm")
            E.op(v.tensor_copy(BT, bank[4][:, 0:P]))
            E.wait("xT", 3)
            E.sync()
            sc3 = scT1.rearrange("p (k n) -> p k n", k=KT)
            sh3 = shT.rearrange("p (k n) -> p k n", k=KT)
            for e in range(2):
                ks = slice(4 * e, 4 * e + 4)
                E.op(v.tensor_tensor(HTv[:, ks, SEQ:R], bank[e][:, 0:32].rearrange("p (k b) -> p k b", k=4), sc3[:, ks, 0:NB], ALU.mult))
            E.sync()
            E.op(v.tensor_tensor(HTv[:, :, SEQ:R], HTv[:, :, SEQ:R], sh3[:, :, 0:NB], ALU.add), "xT_out")

            q.wait_ge(sems("rel_in"), 16)
            E.wait("rows_stored")
            B = RA[:, 0:2048].rearrange("p (h n) -> p h n", h=AH)
            L = RA[:, 2048:4096].rearrange("p (h n) -> p h n", h=AH)
            PT = RA[:, 4096:6144].rearrange("p (h n) -> p h n", h=AH)
            for t in range(NT):
                w = P * (t + 1)
                for h2 in range(4):
                    E.wait("logits")
                    for e in range(2):
                        E.op(v.scalar_tensor_tensor(L[:, 2 * h2 + e, 0:w], bank[LB[2 * (h2 % 2) + e]][:, 0:w], SC_A,
                                                    B[:, 2 * h2 + e, 2 * P - w:2 * P], ALU.mult, ALU.add),
                             "logits_used" if e else None)
                E.sync()
                E.op(v.tensor_reduce(a_mx, L[:, :, 0:w], AX, ALU.max, negate=True), "row_max")
                E.wait("probs")
                E.op(v.reciprocal(a_ri, a_sum))
                if t == 0:
                    q.wait_ge(sems("rel_out"), 16)
                for s in range(t + 1):
                    for hh in range(2):
                        E.wait("probsT")
                        E.op(v.tensor_copy(PT[:, 4 * hh:4 * hh + 4, s * P:(s + 1) * P],
                                           bank[2][:].rearrange("p (e n) -> p e n", e=4)), "probsT_out")
                E.wait("attn_mm")
                E.op(v.tensor_tensor(MIXv[:, t, 0:AW].rearrange("p (h d) -> p h d", h=AH),
                                     bank[3 + t][:].rearrange("p (h d) -> p h d", h=AH),
                                     a_ri.unsqueeze(2).broadcast_to([P, AH, AD]), ALU.mult), "attn_out")
                E.sync()

            q.wait_ge(sems("bgate_in"), 16)
            E.wait("proj_out", 28)
            step(v.tensor_tensor(G3, G3, bg.unsqueeze(1).broadcast_to([P, 3, 8]), ALU.add))
            f3 = lambda x: x.rearrange("p (t n) -> p t n", t=3)
            E.op(v.scalar_tensor_tensor(f3(g_ab), G3[:, :, 4:8], -1.0, G3[:, :, 4:8], ALU.mult, ALU.max), "pre_arg")
            E.op(v.tensor_scalar(f3(g_lf), G3[:, :, 4:8], 0.0, None, ALU.min))
            E.wait("pre_exp")
            E.sync()
            E.op(v.tensor_tensor(g_lf, g_lf, g_ab, ALU.subtract), "logf_ready")
            for c in range(8):
                E.op(v.tensor_scalar(QK[:, c, :], QKT[:, 8 + c, 0:SEQ], cwv[:, c, 3:4], cwv[:, c, 4:5], ALU.mult, ALU.add))
            for j in (2, 1, 0):
                sh = 3 - j
                E.sync()
                for c in range(8):
                    E.op(v.scalar_tensor_tensor(QK[:, c, sh:SEQ], QKT[:, 8 + c, 0:SEQ - sh], cwv[:, c, j:j + 1],
                                                QK[:, c, sh:SEQ], ALU.mult, ALU.add))
            w_of = lambda j: cwv[:, :, j:j + 1].broadcast_to([P, 8, NB])
            state = cwv[:, :, 6:30].rearrange("p c (b j) -> p c b j", j=3)
            step(v.tensor_tensor(YS, QKT[:, 8:16, SEQ:R], w_of(3), ALU.mult))
            step(v.tensor_tensor(YS, YS, w_of(4), ALU.add))
            for j in range(3):
                step(v.tensor_tensor(YT, state[:, :, :, j], w_of(j), ALU.mult))
                step(v.tensor_tensor(YS, YS, YT, ALU.add), "pre_arg" if j == 2 else None)
            E.op(v.memset(ones, 1.0))
            E.wait("pre_exp")
            E8 = RA[:, 2048:4096].rearrange("p (c n) -> p c n", c=8)
            for e in (E8, YT):
                E.op(v.tensor_scalar(e, e, 1.0, None, ALU.add))
            E.sync()
            for e in (E8, YT):
                E.op(v.reciprocal(e, e))
            E.sync()
            for y, e in ((QK, E8), (YS, YT)):
                E.op(v.tensor_tensor(y[:, 0:4, :], y[:, 0:4, :], e[:, 0:4, :], ALU.mult))
                E.op(v.scalar_tensor_tensor(y[:, 4:8, :], y[:, 4:8, :], SC_M, e[:, 4:8, :], ALU.mult, ALU.mult))
            E.sync()
            q.sem_inc(sems("conv_ready"), 1)
            E.wait("pre_exp")
            og, og2 = MIXv[:, 0:2, N:2 * N], MIX[0:NB, 2560:3072]
            for o in (og, og2):
                E.op(v.tensor_scalar(o, o, 1.0, None, ALU.add))
            E.sync()
            for o in (og, og2):
                E.op(v.reciprocal(o, o))
            E.wait("cum")
            step(v.tensor_copy(g_b, bank[0][:, 0:12]))
            step(v.tensor_tensor(f3(g_a), G3[:, :, 0:4], f3(g_b), ALU.subtract))
            step(v.memset(mprev, 0.0))
            eyeb = eye.unsqueeze(1).broadcast_to([P, MH, P])
            bc = lambda x: x.unsqueeze(2).broadcast_to([P, MH, P])
            four = lambda x: x.rearrange("p (h n) -> p h n", h=MH)
            for c in range(2):
                a_c = g_a[:, 4 * c:4 * c + 4]
                E.op(v.tensor_tensor(DG, eyeb, bc(a_c), ALU.mult), "diag_a")
                E.wait("a_rows")
                step(v.tensor_tensor(TM, four(bank[3][:]), cst[:, C_PT:C_PT + P].unsqueeze(1).broadcast_to([P, MH, P]), ALU.add))
                step(v.tensor_reduce(cm, TM, AX, ALU.max))
                step(v.tensor_tensor(bc8[:, 0:4], cm, mprev, ALU.max))
                E.op(v.tensor_copy(bc8[:, 4:8], g_b[:, 4 * c:4 * c + 4]))
                E.op(v.tensor_tensor(DG, eyeb, bc(bc8[:, 0:4]), ALU.mult), "mm_diag")
                E.wait("m_rows")
                E.op(v.tensor_tensor(WT, cst[:, C_PS:C_PS + P].unsqueeze(1).broadcast_to([P, MH, P]), four(bank[4][:]), ALU.subtract))
                E.op(v.tensor_tensor(ex[:, 0:4], mprev, bc8[:, 0:4], ALU.subtract))
                E.op(v.scalar_tensor_tensor(ex[:, 4:8], bc8[:, 4:8], -1.0, bc8[:, 0:4], ALU.mult, ALU.subtract))
                E.wait("last_row")
                E.op(v.tensor_tensor(ex[:, 8:12], a_c, bank[0][:, 16:20], ALU.subtract))
                E.op(v.tensor_tensor(ex[:, 12:16], mprev, bank[0][:, 16:20], ALU.subtract))
                step(v.tensor_copy(mnew, bank[0][:, 16:20]))
                E.op(v.tensor_tensor(mnew, mnew, bank[0][:, 20:24], ALU.add), "ex_args")
                E.wait("wt_ready")
                E.wait("ex_ready")
                E.wait("kq")
                E.op(v.tensor_tensor(ST, four(bank[2][:]), WT, ALU.mult), "st_ready")
                E.op(v.tensor_tensor(WV, four(NAT[:, c, N:2 * N]), bc(ex[:, 8:12]), ALU.mult), "wv_ready")
                mo = MIXv[:, c, N:2 * N]
                E.wait("intra")
                if c == 0:
                    step(v.tensor_copy(den, bank[4][:, 0:4]))
                    num = four(bank[6][:])
                else:
                    E.wait("inter")
                    E.op(v.tensor_tensor(TM, four(bank[5][:]), bc(ex[:, 0:4]), ALU.mult))
                    step(v.tensor_tensor(den, bank[3][:, 0:4], ex[:, 0:4], ALU.mult))
                    E.op(v.tensor_tensor(TM, TM, four(bank[6][:]), ALU.add))
                    step(v.tensor_tensor(den, den, bank[4][:, 0:4], ALU.add))
                    num = TM
                step(v.scalar_tensor_tensor(den, den, -1.0, den, ALU.mult, ALU.max))
                step(v.tensor_tensor(den, den, ex[:, 4:8], ALU.max))
                E.op(v.reciprocal(den, den))
                step(v.tensor_tensor(four(mo), four(mo), num, ALU.mult))
                E.op(v.tensor_tensor(four(mo), four(mo), bc(den), ALU.mult))
                E.wait("state_mm")
                if c == 0:
                    E.op(v.tensor_copy(CT, four(bank[7][:])))
                    E.op(v.tensor_copy(nst, bank[2][:, 0:4]))
                else:
                    E.op(v.tensor_tensor(CT, CT, bc(ex[:, 12:16]), ALU.mult))
                    step(v.tensor_tensor(nst, nst, ex[:, 12:16], ALU.mult))
                    E.op(v.tensor_tensor(CT, CT, four(bank[7][:]), ALU.add))
                    E.op(v.tensor_tensor(nst, nst, bank[2][:, 0:4], ALU.add))
                step(v.tensor_copy(mprev, mnew), "chunk_done")

            E.wait("state_T")
            E.wait("state_stored")
            QD = RA[0:NB, 0:8 * N].rearrange("p (b n) -> p b n", b=NB)
            E.op(v.memset(RA[0:NB, 8 * N:9 * N], 0.0))
            E.op(v.tensor_tensor(QD, SN[0:NB, 0:AW].unsqueeze(1).broadcast_to([NB, NB, AW]),
                                 eye8.unsqueeze(2).broadcast_to([NB, NB, AW]), ALU.mult), "qd_ready")
            q.sem_inc(sems("q_rows_used"), 2)
            E.tally(("made", "q_rows_used")).n = 2
            q.wait_ge(sems("smst_in"), 32)
            tmp = RA[0:NB, 4608:5120]
            step(v.tensor_tensor(tmp, SN[0:NB, 0:AW], SN[0:NB, AW:2 * AW], ALU.mult))
            step(v.tensor_reduce(nl[0:NB, :], tmp.rearrange("p (h d) -> p h d", h=AH), AX, ALU.add))
            step(v.scalar_tensor_tensor(nl[0:NB, :], nl[0:NB, :], SC_A, smst[0:NB, 0:8], ALU.mult, ALU.add))
            E.tally(("made", "blocks_used")).n = BK
            E.tally(("made", "k_logits"))
            with E.loop(4, seen__q_rows=2, made__q_rows_used=2, made__blocks_used=4, seen__lt_T=2, made__dve_steps=2) as i:
                for e in range(2):
                    E.wait("q_rows")
                    E.wait("lt_T")
                    for hf in range(2):
                        n = BK + e * 2 + hf
                        slot = ring[:, n % RING, :].rearrange("p (g n) -> p g n", g=8)
                        q.wait_ge(sems(f"slot{n % RING}"), i * 128 + (before_k[n % RING] + 128))
                        E.op(v.tensor_tensor(slot, slot, bank[e][:].unsqueeze(1).broadcast_to([P, 8, AW]), ALU.mult),
                             "q_rows_used" if hf else None)
                        E.sync()
                        E.op(v.tensor_reduce(LK[e][:, hf * 64:(hf + 1) * 64], slot.rearrange("p g (h d) -> p (g h) d", h=AH),
                                             AX, ALU.add), "blocks_used")
                    E.sync()
                    q.sem_inc(sems("k_logits"), 1)
            E.wait("lt_out", 10)
            step(v.tensor_tensor(LTv, LTv, BT.unsqueeze(1).broadcast_to([P, NB, P]), ALU.add))
            step(v.tensor_reduce(rmx, LTv, AX, ALU.max), "gate_in")
            E.wait("gate_mm")
            W = RA[0:NB, 0:4608]
            g128, gate, c1, c2 = W[:, 0:128], W[:, 128:192], W[:, 512:1024], W[:, 1024:1536]
            rank, am, AM, rm = W[:, 192:256], W[:, 256:320], W[:, 320:448], W[:, 1536:1664]
            NBB = RA[0:NB, 5000:5128]
            step(v.tensor_copy(g128, bank[4][0:NB, 0:P]))
            pages = g128.rearrange("p (n two h) -> p h n two", two=2, h=AH)
            step(v.tensor_tensor(gate.rearrange("p (h n) -> p h n", h=AH), pages[:, :, :, 0], pages[:, :, :, 1], ALU.add))
            gm = gate.rearrange("p (h m) -> p h m", h=AH).unsqueeze(2).broadcast_to([NB, AH, NBLK, NBLK])
            gn = gate.rearrange("p (h n) -> p h n", h=AH).unsqueeze(3).broadcast_to([NB, AH, NBLK, NBLK])
            c14, c24 = (x.rearrange("p (h n m) -> p h n m", h=AH, n=NBLK) for x in (c1, c2))
            low = cst[0:NB, C_LOW:C_LOW + 64].rearrange("p (n m) -> p n m", n=NBLK).unsqueeze(1).broadcast_to([NB, AH, NBLK, NBLK])
            E.op(v.tensor_tensor(c14, gm, gn, ALU.is_gt))
            step(v.tensor_tensor(c24, gm, gn, ALU.is_equal))
            step(v.tensor_tensor(c24, c24, low, ALU.mult))
            step(v.tensor_tensor(c1, c1, c2, ALU.add))
            step(v.tensor_reduce(rank, c1.rearrange("p (x m) -> p x m", m=NBLK), AX, ALU.add))
            step(v.tensor_scalar(am, rank, TOPB - 0.5, NEG, ALU.is_gt, ALU.mult))
            E.op(v.tensor_copy(AM.rearrange("p (n two h) -> p n two h", two=2, h=AH),
                               am.rearrange("p (h n) -> p n h", h=AH).unsqueeze(2).broadcast_to([NB, NBLK, 2, AH])))
            E.sync()
            step(v.tensor_tensor(rm, bank[4][0:NB, P:2 * P], AM, ALU.add))
            step(v.tensor_reduce(m8[0:NB, :], rm.rearrange("p (g h) -> p h g", h=AH), AX, ALU.max))
            step(v.tensor_tensor(m8[0:NB, :], m8[0:NB, :], nl[0:NB, :], ALU.max))
            E.op(v.tensor_tensor(pn[0:NB, :], nl[0:NB, :], m8[0:NB, :], ALU.subtract))
            E.op(v.tensor_tensor(NBB.rearrange("p (g h) -> p g h", h=AH), AM.rearrange("p (g h) -> p g h", h=AH),
                                 m8[0:NB, :].unsqueeze(1).broadcast_to([NB, NPG, AH]), ALU.subtract), "gate_in")
            E.wait("gate_mm")
            step(v.tensor_copy(nbT, bank[4][:, 256:256 + NB]), "nbT_ready")
            with E.loop(4, seen__v_mm=2, made__diag_v=2, made__dve_steps=2) as i:
                for e in range(2):
                    E.wait("v_mm")
                    E.op(v.tensor_copy(SELB[e], cst[0:NB, bass.ds(i * 16 + (C_PICK + 8 * e), 8)]))
                    E.op(v.tensor_tensor(RA[0:NB, e * N:(e + 1) * N].rearrange("p (h d) -> p h d", h=AH),
                                         bank[4 + e][0:NB, :].rearrange("p (h d) -> p h d", h=AH),
                                         eye8.unsqueeze(2).broadcast_to([NB, AH, AD]), ALU.mult), "diag_v")
            E.wait("pn_ready")
            E.wait("gate_mm")
            step(v.tensor_reduce(ri8[0:NB, :], bank[7][0:NB, 0:P].rearrange("p (g h) -> p h g", h=AH), AX, ALU.add))
            step(v.tensor_tensor(ri8[0:NB, :], ri8[0:NB, :], pn[0:NB, :], ALU.add))
            E.op(v.reciprocal(ri8[0:NB, :], ri8[0:NB, :]))
            at8 = MIX[0:NB, 2048:2560].rearrange("p (h d) -> p h d", h=AH)
            b8 = lambda x: x[0:NB, :].unsqueeze(2).broadcast_to([NB, AH, AD])
            step(v.tensor_tensor(at8, SN[0:NB, 1024:1536].rearrange("p (h d) -> p h d", h=AH), b8(pn), ALU.mult))
            E.wait("v_sum", 8)
            step(v.tensor_tensor(at8, at8, bank[6][0:NB, :].rearrange("p (h d) -> p h d", h=AH), ALU.add))
            step(v.tensor_tensor(at8, at8, b8(ri8), ALU.mult))
            q.sem_inc(sems("satt_done"), 1)

            lf8, i8 = g_lf[0:NB, 8:12], G3[0:NB, 2, 0:4]
            S = sE[0:NB, :]
            step(v.tensor_tensor(S[:, 0:4], lf8, smst[0:NB, 8:12], ALU.add))
            step(v.tensor_tensor(sM[0:NB, :], S[:, 0:4], i8, ALU.max))
            E.op(v.tensor_tensor(S[:, 4:8], i8, sM[0:NB, :], ALU.subtract))
            E.op(v.tensor_scalar(S[:, 8:12], sM[0:NB, :], -1.0, None, ALU.mult))
            step(v.tensor_tensor(S[:, 0:4], S[:, 0:4], sM[0:NB, :], ALU.subtract), "sE_args")
            E.wait("sE_ready")
            h8 = lambda x: x.rearrange("p (h n) -> p h n", h=MH)
            b4 = lambda x: x.unsqueeze(2).broadcast_to([NB, MH, P])
            E.op(v.tensor_tensor(KQW.rearrange("p (b h) -> p b h", b=NB), S[:, 0:4].unsqueeze(1).broadcast_to([NB, NB, MH]),
                                 eye8.unsqueeze(2).broadcast_to([NB, NB, MH]), ALU.mult), "smem_in")
            E.op(v.tensor_tensor(h8(EV), h8(SN[0:NB, 1536:2048]), b4(S[:, 4:8]), ALU.mult), "smem_in")
            q.wait_ge(sems("ns_in"), 16)
            E.wait("kqn_out")
            T8 = SN[0:NB, 512:1024]
            step(v.tensor_tensor(h8(NS), h8(NS), b4(S[:, 0:4]), ALU.mult))
            step(v.tensor_tensor(h8(T8), h8(KQN[:, 0:N]), b4(S[:, 4:8]), ALU.mult))
            step(v.tensor_tensor(NS, NS, T8, ALU.add))
            step(v.tensor_tensor(T8, NS, KQN[:, N:2 * N], ALU.mult))
            step(v.tensor_reduce(den[0:NB, :], h8(T8), AX, ALU.add))
            step(v.scalar_tensor_tensor(den[0:NB, :], den[0:NB, :], -1.0, den[0:NB, :], ALU.mult, ALU.max))
            step(v.tensor_tensor(den[0:NB, :], den[0:NB, :], S[:, 8:12], ALU.max))
            step(v.reciprocal(den[0:NB, :], den[0:NB, :]))
            E.wait("smem_mm")
            E.op(v.tensor_copy(wcB, bank[2][:, 0:32]))
            E.wait("smem_mm")
            step(v.tensor_copy(evT, bank[3][:, 0:32]), "ev_out")
            q.wait_ge(sems("cs_in"), 16)
            T4 = HT[:, 0:512].rearrange("p (h n) -> p h n", h=MH)
            for b in range(NB):
                C = CS[:, b, :, :]
                E.wait("kq_rows")
                E.op(v.tensor_tensor(C, C, wcB[:, 4 * b:4 * b + 4].unsqueeze(2).broadcast_to([P, MH, P]), ALU.mult))
                step(v.tensor_tensor(T4, four(bank[b % 2][:]), evT[:, b:b + 25:8].unsqueeze(2).broadcast_to([P, MH, P]), ALU.mult))
                step(v.tensor_tensor(C, C, T4, ALU.add))
                step(v.tensor_tensor(T4, C, four(bank[4 + b % 2][:]), ALU.mult), "kq_used")
                step(v.tensor_reduce(numS[:, b:b + 25:8], T4, AX, ALU.add))
            q.sem_inc(sems("c_new"), 1)
            E.wait("smem_mm")
            o8 = MIX[0:NB, 2560:3072]
            step(v.tensor_tensor(o8, o8, bank[3][0:NB, :], ALU.mult))
            step(v.tensor_tensor(h8(o8), h8(o8), b4(den[0:NB, :]), ALU.mult))
            q.sem_inc(sems("smem_done"), 1)

            q.wait_ge(sems("ln1_in"), 32)
            E.wait("mixT_out", 3)
            E.wait("y_mm", 2)
            E.wait("bc_out", 3)
            E.op(v.memset(QT[:, 16, :, 64:P], 0.0), "qt_zero")
            for t in range(3):
                rows = P if t < 2 else NB
                sl = slice(0, rows)
                vec = lambda n, col: RA[sl, 2048 + n * DM:3072 + n * DM] if t < 2 else MOD[sl, col:col + DM]
                x, y, h2 = Xv[sl, t, :], MIXv[sl, t, :], H2[sl, t, :]
                g1 = vec(0, 2 * DM)
                for e in range(2):
                    E.op(v.tensor_tensor(y[:, e * N:(e + 1) * N], bank[3 * e + t][sl, :], g1[:, e * N:(e + 1) * N], ALU.mult))
                E.sync()
                step(v.scalar_tensor_tensor(y, x, ALPHA, y, ALU.mult, ALU.add))
                norm_rows(E, t, y, rows, y)
                E.sync()
                step(v.tensor_tensor(y, y, RA[sl, 0:DM], ALU.mult))
                step(v.tensor_tensor(x, y, RA[sl, DM:2 * DM], ALU.add))
                norm_rows(E, t, x, rows, h2)
                E.sync()
                step(v.scalar_tensor_tensor(h2, vec(1, 4 * DM), 1.0, h2, ALU.add, ALU.mult))
                E.op(v.tensor_tensor(h2, h2, vec(2, 3 * DM), ALU.add), "h2_ready")

            E.op(v.memset(MIX[0:NB, 2048:2560], 0.0), "zeros_ready")
            q.sem_inc(sems("u_slot_free"), UR)
            q.sem_inc(sems("diag_w"), 2 * PK)
            q.sem_inc(sems("scores_used"), 1)
            E.tally(("made", "u_slot_free")).n = UR
            E.tally(("made", "scores_used")).n = 1
            E.tally(("seen", "v_slot_free")).n = UR - PK
            E.tally(("seen", "scores")).n = 1

            def topk(par, first=False):
                E.wait("scores")
                E.hold()
                half_s = [bank[0][:, e * P:(e + 1) * P] for e in range(2)]
                lo = lambda e: slice(e * PK, e * PK + 8)
                hi = lambda e: slice(e * PK + 8, e * PK + 16)
                for e in range(2):
                    E.op(v.max(v2[:, lo(e)], half_s[e]))
                E.sync()
                E.hold()
                for e in range(2):
                    E.op(v.match_replace(TMPS[:, e * P:(e + 1) * P], v2[:, lo(e)], half_s[e], -3e38))
                E.sync()
                E.hold()
                for e in range(2):
                    E.op(v.max(v2[:, hi(e)], TMPS[:, e * P:(e + 1) * P]))
                for e in range(2):
                    E.op(v.max_index(ixu[:, lo(e)], v2[:, lo(e)], half_s[e]), "scores_used" if e else None)
                E.sync()
                E.hold()
                for e in range(2):
                    E.op(v.max_index(ixu[:, hi(e)], v2[:, hi(e)], TMPS[:, e * P:(e + 1) * P]))
                cand3 = CAND.rearrange("p (i j) -> p i j", i=PK)
                step(v.tensor_tensor(cand3, v2[:, 0:PK].unsqueeze(2).broadcast_to([P, PK, PK]),
                                     v2[:, PK:2 * PK].unsqueeze(1).broadcast_to([P, PK, PK]), ALU.add))
                E.op(v.tensor_copy(i2f, ixu[:, 0:2 * PK]))
                b_ = bs[par]
                E.sync()
                E.hold()
                step(v.max(b_[:, 0:8], CAND))
                E.hold()
                E.op(v.match_replace(CAND2, b_[:, 0:8], CAND, -3e38))
                E.op(v.max_index(ixu[:, 2 * PK:2 * PK + 8], b_[:, 0:8], CAND))
                E.sync()
                E.hold()
                step(v.max(b_[:, 8:16], CAND2))
                E.op(v.tensor_scalar(nbs[par], b_[:, 0:1], -1.0, None, ALU.mult), "best_ready")
                step(v.max_index(ixu[:, 2 * PK + 8:3 * PK], b_[:, 8:16], CAND2))
                E.op(v.tensor_scalar(ixu[:, 3 * PK:4 * PK], ixu[:, 2 * PK:3 * PK], 4, None, ALU.logical_shift_right))
                step(v.tensor_scalar(ixu[:, 4 * PK:5 * PK], ixu[:, 2 * PK:3 * PK], 15, None, ALU.bitwise_and))
                step(v.tensor_copy(abf, ixu[:, 3 * PK:5 * PK]))
                OH3 = OH.rearrange("p (s c) -> p s c", c=PK)
                step(v.tensor_tensor(OH3, cst[:, C_IOTA:C_IOTA + PK].unsqueeze(1).broadcast_to([P, 2 * PK, PK]),
                                     abf.unsqueeze(2).broadcast_to([P, 2 * PK, PK]), ALU.is_equal))
                OH4 = OH.rearrange("p (s k c) -> p s k c", s=2, c=PK)
                step(v.tensor_tensor(OH4, OH4, i2f.rearrange("p (s c) -> p s c", s=2).unsqueeze(2).broadcast_to([P, 2, PK, PK]), ALU.mult))
                step(v.tensor_reduce(selk, OH3, AX, ALU.add))
                if not first:
                    E.wait("v_slot_free", PK)
                step(v.scalar_tensor_tensor(tok[:, par * PK:(par + 1) * PK], selk[:, 0:PK], float(NK), selk[:, PK:2 * PK],
                                            ALU.mult, ALU.add), "idx_ready")

            def head(par, rows, h2, base, i=None):
                w = wS[par][0:rows, :]
                for k in range(PK):
                    s = k % UR
                    count = 16 * (base + par * 2 + k // UR + 1)
                    q.wait_ge(sems(f"u{s}_in"), count if i is None else i * 64 + count)
                    u = ring_t[0:rows, s * DM:(s + 1) * DM]
                    E.op(v.tensor_tensor_reduce(out=u, in0=u, in1=h2, scale=1.0, scalar=0.0, op0=ALU.mult, op1=ALU.add,
                                                accum_out=w[:, k:k + 1]), "u_slot_free")
                E.sync()
                x, y = wA[0:rows, :], wB[0:rows, :]
                step(v.tensor_tensor(x, w, w, ALU.mult))
                step(v.tensor_scalar(x, x, 0.044715, 1.0, ALU.mult, ALU.add))
                step(v.tensor_tensor(y, x, w, ALU.mult))
                step(v.tensor_scalar(y, y, -2.0 * GC, 80.0, ALU.mult, ALU.min), "gelu_arg")
                E.wait("best_exp")
                step(v.reciprocal(er[0:rows, :], esum[par][0:rows, :]))
                step(v.tensor_scalar(x, ebs[par][0:rows, :], er[0:rows, :], None, ALU.mult))
                step(v.tensor_tensor(x, x, w, ALU.mult))
                E.wait("gelu_exp")
                step(v.tensor_scalar(y, y, 1.0, None, ALU.add))
                step(v.reciprocal(y, y))
                E.wait("diag_w", PK)
                E.op(v.tensor_tensor(wG[par][0:rows, :], x, y, ALU.mult), "w_ready")

            E.wait("sk_out")
            E.wait("g2_out")
            topk(0, True)
            for t in range(NT):
                with E.loop(PH // 2, seen__scores=2, made__scores_used=2, made__best_ready=2, made__idx_ready=2,
                            seen__v_slot_free=2 * PK, made__u_slot_free=2 * PK, made__gelu_arg=2, seen__best_exp=2,
                            seen__gelu_exp=2, seen__diag_w=2 * PK, made__w_ready=2, made__dve_steps=60) as i:
                    for par in range(2):
                        head(par, P, H2[:, t, :], t * 2 * PH, i)
                        topk(1 - par)
            head(0, AH * NB, RA[0:AH * NB, 5120:6144], 4 * PH)

            q.wait_ge(sems("ln2_in"), 32)
            for t in range(3):
                rows = P if t < 2 else NB
                sl = slice(0, rows)
                E.wait("f_ready")
                g2 = RA[sl, 2048:3072] if t < 2 else MOD[sl, 5 * DM:6 * DM]
                x, y = Xv[sl, t, :], SN[sl, 0:DM]
                for e in range(2):
                    E.op(v.tensor_tensor(y[:, e * N:(e + 1) * N], bank[(4, 6, 2)[t] + e][sl, :], g2[:, e * N:(e + 1) * N], ALU.mult))
                E.sync()
                step(v.scalar_tensor_tensor(y, x, ALPHA, y, ALU.mult, ALU.add))
                norm_rows(E, t, y, rows, y)
                E.sync()
                step(v.tensor_tensor(y, y, RA[sl, 0:DM], ALU.mult))
                step(v.tensor_tensor(x, y, RA[sl, DM:2 * DM], ALU.add))
                q.sem_inc(sems("y_ready"), 1)


INS = ["x_prompt", "x_sample", "cache_k", "cache_v", "page_table", "state_C", "state_n", "state_m", "state_conv",
       "c_prompt", "c_sample", "rel_bias_table", "w_ada", "b_ada", "w_in", "b_gate", "conv_w", "conv_b",
       "beta_attn", "beta_mlstm", "w_out", "ln1_g", "ln1_b", "w_query", "sub_keys", "expert_u", "expert_v",
       "ln2_g", "ln2_b"]
OUTS = [("y_prompt", (1, SEQ, DM)), ("y_sample", (NB, 1, DM)),
        ("k_prompt", (1, 1, SEQ, AH, AD)), ("v_prompt", (1, 1, SEQ, AH, AD)),
        ("C_prompt", (1, 1, MH, MD, MD)), ("n_prompt", (1, 1, MH, MD)), ("m_prompt", (1, 1, MH)),
        ("conv_prompt", (1, 1, CW - 1, 2 * MW)),
        ("k_sample", (1, NB, 1, AH, AD)), ("v_sample", (1, NB, 1, AH, AD)),
        ("C_sample", (1, NB, MH, MD, MD)), ("n_sample", (1, NB, MH, MD)), ("m_sample", (1, NB, MH)),
        ("conv_sample", (1, NB, CW - 1, 2 * MW))]


def kernel(**inputs):
    import concourse.bacc as bacc
    from concourse.bass_utils import run_bass_kernel_spmd

    nc = bacc.Bacc("TRN2", target_bir_lowering=False, num_devices=1)
    arrays = {n: np.ascontiguousarray(inputs[n]) for n in INS}
    arrays["consts"], arrays["onehot"] = constants()
    A = {n: nc.dram_tensor(f"in_{n}", a.shape, mybir.dt.from_np(a.dtype), kind="ExternalInput").ap() for n, a in arrays.items()}
    O = {n: nc.dram_tensor(f"out_{n}", s, F32, kind="ExternalOutput").ap() for n, s in OUTS}
    build(nc, A, O)
    r = run_bass_kernel_spmd(nc, [{f"in_{n}": a for n, a in arrays.items()}], core_ids=[0])
    return tuple(r.results[0][f"out_{n}"] for n, _ in OUTS)
```

```python
from contextlib import ExitStack, contextmanager

import numpy as np

import concourse.bass as bass
from concourse import mybir

F32 = mybir.dt.float32
U32 = mybir.dt.uint32
I32 = mybir.dt.int32
ALU = mybir.AluOpType
ACT = mybir.ActivationFunctionType
AX = mybir.AxisListType.X

P = 128
DM = 1024
KT = DM // P
SEQ = 256
NT = SEQ // P
NB = 8
R = SEQ + NB
AH, AD = 8, 64
AW = AH * AD
MH, MD = 4, 128
MW = MH * MD
NPG = 16
PG = 128
NBLK = 8
TOPB = 3
NBUCK = 32
CW = 4
PH = 8
PK = 16
NK = 128
N = 512
ALPHA = 2.0 ** 0.25
SC_A = AD ** -0.5
SC_M = MD ** -0.5
EPS = 1e-5
NEG = -1e30
GC = 0.7978845608028654
RING = 4
ROWS_AT = {9: 2, 12: 3, 16: 4, 20: 5, 23: 6, 25: 7}
RPITCH = 384
UR = 8
TRIPS = (PH // 2, PH // 2 - 1)
BASE = (0, 2 * PH + 2)


def constants():
    eye = np.eye(P, dtype=np.float32)
    s = np.arange(P)
    upto = (s[:, None] <= s[None, :]).astype(np.float32)
    past_t = np.where(s[None, :] <= s[:, None], 0.0, NEG)
    past_s = np.where(s[:, None] <= s[None, :], 0.0, NEG)
    head_sum = np.zeros((P, NB))
    for p in range(AH * NB):
        head_sum[p, p % NB] = 1.0
    pick = np.tile(np.eye(NB).reshape(-1), (P, 1))
    lower = np.zeros((P, NBLK * NBLK))
    for n in range(NBLK):
        lower[:, n * NBLK:n * NBLK + n] = 1.0
    again = np.tile(np.eye(P, NB), (1, AH))
    iota = np.tile(np.arange(PK), (P, 1))
    rows_of = np.zeros((P, 2 * NB))
    own = np.zeros((P, AH))
    for b in range(NB):
        for h in range(AH):
            rows_of[32 * (b % 4) + h, NB * (b // 4) + b] = 1.0
            own[32 * (b % 4) + h, h] = 1.0
    cst = np.concatenate([eye, upto, past_t, past_s, head_sum, pick, lower, iota, again, rows_of, own], 1)

    def bucket(d):
        d = np.maximum(d, 0)
        far = 16 + (np.log(np.maximum(d, 1) / 16.0) / np.log(8.0) * 16).astype(np.int64)
        return np.where(d < 16, d, np.minimum(far, NBUCK - 1))

    dist = 255 - np.arange(RPITCH)
    one = np.zeros((NBUCK + 1, RPITCH + PG))
    one[bucket(dist), np.arange(RPITCH)] = dist >= 0
    one[NBUCK, :RPITCH] = dist < 0
    last = PG - np.arange(PG)
    one[bucket(last), RPITCH + np.arange(PG)] = 1.0
    return cst.astype(np.float32), one.astype(np.float32)


C_EYE, C_UPTO, C_PT, C_PS = 0, 128, 256, 384
C_HS, C_PICK, C_LOW, C_IOTA = 512, 520, 584, 648
C_REP = C_IOTA + PK
C_SUM = C_REP + 64
C_OWN = C_SUM + 16
C_ALL = C_OWN + 8


def v_col(s):
    return (s + UR // 2) % UR * DM


def u_col(s):
    return (UR + (s + UR // 2) % UR) * DM


class Tally:

    def __init__(self):
        self.n, self.var = 0, None

    def add(self, k):
        self.n += k
        return self.at()

    def at(self):
        return self.n if self.var is None else self.var + self.n


class Engine:

    def __init__(self, q, sems, name):
        self.q, self.sems, self.name = q, sems, name
        self.tallies, self.last = {}, None

    def tally(self, key):
        return self.tallies.setdefault(key, Tally())

    def sem(self, name):
        return self.sems(name)

    def op(self, ins, name=None, n=1):
        name = name or self.name + "_steps"
        ins.then_inc(self.sem(name), n)
        self.last = (name, self.tally(("made", name)).add(n))
        return ins

    def sync(self):
        self.q.wait_ge(self.sem(self.last[0]), self.last[1])

    def wait(self, name, n=1):
        self.q.wait_ge(self.sem(name), self.tally(("seen", name)).add(n))

    def hold(self):
        self.q.sem_inc(self.sem(self.name + "_go"), 1)

    @contextmanager
    def loop(self, trips, **per):
        keys = {(k.split("__")[0], k.split("__")[1]): v for k, v in per.items()}
        with self.q.Fori(0, trips) as i:
            start = {k: self.tally(k).n for k in keys}
            others = {k: t.n for k, t in self.tallies.items() if k not in keys}
            for k, v in keys.items():
                self.tally(k).var = i * v
            yield i
            for k, v in keys.items():
                t = self.tally(k)
                assert t.n - start[k] == v, (self.name, k, t.n - start[k], v)
            for k, t in self.tallies.items():
                assert k in keys or others.get(k, 0) == t.n, (self.name, k, "moves in a loop")
        for k, v in keys.items():
            t = self.tally(k)
            t.var, t.n = None, start[k] + trips * v
        if self.last:
            self.last = (self.last[0], self.tally(("made", self.last[0])).at())


def build(nc, A, O):
    ctx = ExitStack()
    with ctx:
        made = {}

        def sems(name):
            if name not in made:
                made[name] = ctx.enter_context(nc.semaphore(name))
            return made[name]

        def sb(name, cols, dt=F32, rows=P):
            return ctx.enter_context(nc.sbuf_tensor(name, [rows, cols], dt))

        def dram(name, shape):
            return nc.dram_tensor(name, shape, F32, kind="Internal").ap()

        ring_t = sb("ring", RING * 4096)
        MOD = sb("mod", 6144)
        X = sb("x", 3 * DM)
        HT = sb("ht", KT * R)
        R1 = sb("r1", 17 * 256 + 3 * DM)
        SN = sb("sn", 2560)
        RA = sb("ra", 6144)
        MIX = sb("mix", 3 * DM)
        LT = sb("lt", NB * PG)
        W2 = sb("w2", 1024)
        cst = sb("cst", C_ALL)
        sm = sb("small", 1200)
        tok = sb("idx", 2 * PK, U32)
        ixu = sb("topi", 5 * PK, U32)
        ptab = sb("ptab", NB * NPG, I32)

        eye = cst[:, C_EYE:C_EYE + P]
        eye8 = cst[0:NB, C_EYE:C_EYE + NB]
        upto = cst[:, C_UPTO:C_UPTO + P]
        ring = ring_t[:].rearrange("p (s n) -> p s n", s=RING)
        Xv = X[:].rearrange("p (t n) -> p t n", t=3)
        HTv = HT[:].rearrange("p (k r) -> p k r", k=KT)
        QKT = R1[:, 0:16 * R].rearrange("p (c r) -> p c r", c=16)
        NAT = R1[:, 16 * R:16 * R + 3 * 2 * N].rearrange("p (t n) -> p t n", t=2)
        H2 = R1[:, 0:3 * DM].rearrange("p (t n) -> p t n", t=3)
        QT = R1[:, 3 * DM:3 * DM + 17 * 256].rearrange("p (i s r) -> p i s r", i=17, s=2)
        MIXv = MIX[:].rearrange("p (t n) -> p t n", t=3)
        LTv = LT[:].rearrange("p (b n) -> p b n", b=NB)
        BT = W2[:, 0:P]
        LK = [W2[:, P * (1 + e):P * (2 + e)] for e in range(2)]
        WG8 = W2[:, 3 * P:3 * P + 64]
        YS, YT = (W2[:, 4 * P + 64 * e:4 * P + 64 * (e + 1)].rearrange("p (c b) -> p c b", c=8) for e in range(2))
        SKN, SKT = LT[:, 0:256], LT[:, 256:512]
        TMPS, CAND = LT[:, 512:768], LT[:, 768:1024]
        CAND2, OH, QS = W2[:, 0:256], W2[:, 256:768], W2[:, 768:1024]

        at = [0]

        def small(cols):
            at[0] += cols
            assert at[0] <= 1200
            return sm[:, at[0] - cols:at[0]]

        shT, scT1, silT = small(72), small(72), small(72)
        cwT = small(8 * 30)
        cwv = cwT.rearrange("p (c n) -> p c n", c=8)
        G, bg = small(24), small(8)
        G3 = G.rearrange("p (t n) -> p t n", t=3)
        g_ab, g_lf, g_b, g_a = (small(12) for _ in range(4))
        stats = small(3 * 12)
        mv = small(3 * 2)
        rstd = small(3)
        half = small(1)
        a_mx, a_sum, a_ri = small(8), small(8), small(8)
        cm, mprev, mnew, den, den2 = (small(4) for _ in range(5))
        ex = small(16)
        bc8 = small(8)
        nst = small(4)
        tab = small(8)
        gs, rmx, rs, nbT = small(8), small(8), small(8), small(8)
        nl, m8, pn, ri8 = small(8), small(8), small(8), small(8)
        sM = small(4)
        sE = small(12)
        st12 = small(12)
        wcB = small(32)
        evT = small(32)
        numS = small(32)
        smst = small(12)
        wS = [small(PK) for _ in range(2)]
        wA, wB, wG = small(PK), small(PK), [small(PK) for _ in range(2)]
        v2 = small(2 * PK)
        i2f = small(2 * PK)
        bs = [small(PK) for _ in range(2)]
        nbs = [small(1) for _ in range(2)]
        ebs = [small(PK) for _ in range(2)]
        esum = [small(1) for _ in range(2)]
        er = small(1)
        abf = small(2 * PK)
        selk = small(2 * PK)

        bank = [ctx.enter_context(nc.psum_tensor(f"bank{i}", [P, N], F32)) for i in range(8)]

        KQ_BANKS = ((5, 6), (1, 3))

        ones8 = cst[0:NB, C_UPTO + NB - 1:C_UPTO + NB].broadcast_to([NB, P])

        LB = (0, 1, 5, 6)

        rel = dram("rel_rows", (AH, P, RPITCH))
        mods = dram("prompt_mods", (1, 6 * DM))

        T4 = R1[:, 16 * R:16 * R + N].rearrange("p (h n) -> p h n", h=MH)
        KQW = R1[0:NB, 16 * R + N:16 * R + N + 32]
        VO = R1[:, 16 * R + 2 * N:16 * R + 4 * N].rearrange("p (e n) -> p e n", e=2)
        QK = HT[:, 0:2048].rearrange("p (c n) -> p c n", c=8)
        E8 = ring[:, 0, 0:2048].rearrange("p (c n) -> p c n", c=8)
        TAP = ring[:, 0, 2048:4096].rearrange("p (c n) -> p c n", c=8)
        KN = RA[:, 2048:2560].rearrange("p (h n) -> p h n", h=MH)
        CT = RA[:, 2560:3072].rearrange("p (h n) -> p h n", h=MH)
        WT = RA[:, 3072:3584].rearrange("p (h n) -> p h n", h=MH)
        ST = RA[:, 3584:4096].rearrange("p (h n) -> p h n", h=MH)
        WV = RA[:, 4096:4608].rearrange("p (h n) -> p h n", h=MH)
        DG = RA[:, 4608:5120].rearrange("p (h n) -> p h n", h=MH)
        TM = RA[:, 5120:5632].rearrange("p (h n) -> p h n", h=MH)
        ones = RA[:, 5632:5760]
        CS = RA[:, 2048:6144].rearrange("p (b h k) -> p b h k", b=NB, h=MH)
        GV = ring[:, 2, 0:3 * DM]
        KQN = W2[0:NB, :]
        EV = SN[0:NB, 2048:2560]
        NS = SN[0:NB, 0:512]
        BO, BQ = 19, 21
        SLOT = [n % 2 for n in range(BQ + 2)] + [3, 2]

        def block_sem(n):
            return (f"slot{n % 2}", 16 * (n // 2 + 1)) if n < BQ + 2 else (f"late{n % 2}", 16)

        def norm_rows(E, t, src, rows, dst, name=None, var="var_ready", root="rstd_ready"):
            v = nc.vector
            for e in range(2):
                E.op(v.bn_stats(stats[0:rows, t * 12 + 6 * e:t * 12 + 6 * e + 6], src[:, e * N:(e + 1) * N]))
            E.sync()
            E.op(v.bn_aggr(mv[0:rows, 2 * t:2 * t + 2], stats[0:rows, t * 12:t * 12 + 12].rearrange("p (e n) -> p e n", e=2)))
            E.sync()
            E.op(v.tensor_scalar(mv[0:rows, 2 * t + 1:2 * t + 2], mv[0:rows, 2 * t + 1:2 * t + 2], EPS, None, ALU.add), var)
            E.wait(root)
            E.op(v.tensor_scalar(dst, src, mv[0:rows, 2 * t:2 * t + 1], rstd[0:rows, t:t + 1], ALU.subtract, ALU.mult), name)

        block = ctx.enter_context(nc.Block())

        @block.sync
        def _(q):
            def load(dst, src, name):
                q.dma_start(dst, src).then_inc(sems(name), 16)

            def weights(n, w, j):
                if 2 <= n < BQ + 2:
                    q.wait_ge(sems("blocks_used"), n - 1)
                load(ring[:, SLOT[n], :].rearrange("p (k n) -> p k n", k=KT), w[:, :, j * N:(j + 1) * N], block_sem(n)[0])

            load(RA[0:NB, 0:DM], A["c_sample"], "c_in")
            load(RA[NB:NB + 1, 0:DM], A["c_prompt"], "c_in")
            load(cst[:], A["consts"], "consts_in")
            w_ada = A["w_ada"].rearrange("o (k p) n -> (o p) k n", p=P)
            w_in = A["w_in"].rearrange("o (k p) n -> (o p) k n", p=P)
            for n in range(12):
                weights(n, w_ada, n)
                if n == 0:
                    load(MOD[0:9, :], A["b_ada"].partition_broadcast(9), "bada_in")
                    load(Xv[:, 0:2, :], A["x_prompt"].rearrange("o (t p) d -> (o p) t d", p=P), "x_in")
                    load(Xv[0:NB, 2, :], A["x_sample"].rearrange("b o d -> (b o) d"), "x_in")
                if n == 1:
                    cw = RA[:, 1024:2048]
                    load(cw[0:4, :], A["conv_w"].rearrange("o j c -> (o j) c"), "cw_in")
                    load(cw[4:5, :], A["conv_b"], "cw_in")
                    load(cw[5:6, 0:AW], A["beta_attn"], "cw_in")
                    load(cw[5:6, AW:DM], A["beta_mlstm"], "cw_in")
                    load(cw[6:30, :], A["state_conv"].rearrange("o b j c -> (o b j) c"), "cw_in")
                    load(RA[0:NBUCK + 1, 2048:2048 + RPITCH + PG], A["onehot"], "tab_in")
                    load(tab[0:NBUCK, :], A["rel_bias_table"], "tab_in")
                    load(WG8.rearrange("p (k n) -> p k n", k=KT), w_in[:, :, 7 * N:7 * N + 8], "wg_in")
                    load(bg, A["b_gate"].partition_broadcast(P), "bgate_in")
                    load(ptab[0:1, :], A["page_table"].rearrange("b n -> (b n)").unsqueeze(0), "ptab_in")
                    load(smst[0:NB, 0:8], A["rel_bias_table"][0:1, :].partition_broadcast(NB), "smst_in")
                    load(smst[0:NB, 8:12], A["state_m"].rearrange("o b h -> (o b) h"), "smst_in")
            for j in range(2):
                weights(12 + j, w_in, j)

            q.wait_ge(sems("rel_ready"), 1)
            q.dma_start(rel, RA[0:AH, 4096:4096 + RPITCH].unsqueeze(1).broadcast_to([AH, P, RPITCH])).then_inc(sems("rel_out"), 16)
            q.wait_ge(sems("rel_out"), 16)
            skew = bass.AP(rel.tensor, P - 1, [[RPITCH - 1, P], [P * RPITCH, AH], [1, 2 * P]])
            q.wait_ge(sems("cwT_ready"), 1)
            load(RA[:, 0:2048].rearrange("p (h n) -> p h n", h=AH), skew, "rel_in")

            q.wait_ge(sems("ptab_in"), 16)
            for pool, base in ((A["cache_k"], 0), (A["cache_v"], 16)):
                pages = pool.rearrange("o g r h d -> (o g) r (h d)")
                with q.Fori(0, 4) as i:
                    for j in range(4):
                        q.wait_ge(sems("kv_used"), i * 4 + (base + j + 1))
                        for g in range(8):
                            page = q.value_load(ptab[0:1, bass.ds(i * 32 + (j * 8 + g), 1)])
                            q.dma_start(ring[:, 2 + j % 2, g * N:(g + 1) * N],
                                        pages[bass.ds(page, 1), :, :].rearrange("g r n -> (g r) n")
                                        ).then_inc(sems(f"kv{j % 2}"), 16)
            w_q = A["w_query"].rearrange("o (k p) n -> (o p) k n", p=P)
            q.wait_ge(sems("attn_out"), 2)
            load(RA[:, 0:DM], A["ln1_g"].partition_broadcast(P), "ln1_in")
            load(RA[:, DM:2 * DM], A["ln1_b"].partition_broadcast(P), "ln1_in")
            q.wait_ge(sems("kv_used"), 34)
            q.wait_ge(sems("mods_out"), 16)
            for v, n in enumerate((2, 4, 3)):
                load(GV[:, v * DM:(v + 1) * DM], mods[0:1, n * DM:(n + 1) * DM].partition_broadcast(P), "ln1_in")
            load(SKN.rearrange("p (s d) -> p s d", s=2), A["sub_keys"].rearrange("o s n d -> (o n) s d"), "sk_in")
            weights(BQ + 2, w_q, 2)
            for j in range(2):
                weights(BQ + j, w_q, j)
            q.wait_ge(sems("h2_ready"), 3)
            weights(BQ + 3, w_q, 3)
            load(RA[:, 0:DM], A["ln2_g"].partition_broadcast(P), "ln2_in")
            load(RA[:, DM:2 * DM], A["ln2_b"].partition_broadcast(P), "ln2_in")
            q.wait_ge(sems("cs_stored"), 16)
            load(RA[:, 2 * DM:3 * DM], mods[0:1, 5 * DM:6 * DM].partition_broadcast(P), "ln2_in")

        @block.gpsimd
        def _(q):
            E = Engine(q, sems, "pool")
            g = nc.gpsimd
            E.op(g.memset(half[:], -0.5))
            E.op(g.memset(W2[:, 3 * P + 64:4 * P], 0.0))
            E.op(g.memset(W2[:, 5 * P:], 0.0), "w2_zero")
            E.sync()

            def rsqrt(t):
                rows = P if t < 2 else NB
                E.wait("var_ready")
                E.op(g.tensor_tensor(rstd[0:rows, t:t + 1], mv[0:rows, 2 * t + 1:2 * t + 2], half[0:rows, :], ALU.pow), "rstd_ready")

            for t in range(3):
                rsqrt(t)
            def step(ins, name=None):
                E.op(ins, name)
                E.sync()

            q.wait_ge(sems("proj_out"), 28)
            q.wait_ge(sems("cwT_ready"), 1)
            for c in range(8):
                E.op(g.tensor_scalar(QK[:, c, :], QKT[:, 8 + c, 0:SEQ], cwv[:, c, 3:4], cwv[:, c, 4:5], ALU.mult, ALU.add))
            for j in (2, 1, 0):
                sh = 3 - j
                step(g.tensor_tensor(TAP[:, :, 0:SEQ - sh], QKT[:, 8:16, 0:SEQ - sh],
                                     cwv[:, :, j:j + 1].broadcast_to([P, 8, SEQ - sh]), ALU.mult))
                step(g.tensor_tensor(QK[:, :, sh:SEQ], QK[:, :, sh:SEQ], TAP[:, :, 0:SEQ - sh], ALU.add))
            w_of = lambda j: cwv[:, :, j:j + 1].broadcast_to([P, 8, NB])
            state = cwv[:, :, 6:30].rearrange("p c (b j) -> p c b j", j=3)
            step(g.tensor_tensor(YS, QKT[:, 8:16, SEQ:R], w_of(3), ALU.mult))
            step(g.tensor_tensor(YS, YS, w_of(4), ALU.add))
            for j in range(3):
                step(g.tensor_tensor(YT, state[:, :, :, j], w_of(j), ALU.mult))
                step(g.tensor_tensor(YS, YS, YT, ALU.add), "conv_arg" if j == 2 else None)
            E.wait("sigm_ready")
            for y, e in ((QK, E8), (YS, YT)):
                E.op(g.tensor_tensor(y, y, e, ALU.mult))
            E.sync()
            for y in (QK, YS):
                E.op(g.tensor_scalar(y[:, 4:8, :], y[:, 4:8, :], SC_M, None, ALU.mult))
            E.sync()
            q.sem_inc(sems("conv_ready"), 1)

            for t in range(3):
                rsqrt(t)
                rsqrt(t)

            eu = A["expert_u"].rearrange("o e d -> (o e) d")
            ev = A["expert_v"].rearrange("o e d -> (o e) d")

            def head(par, rows):
                E.wait("idx_ready")
                E.hold()
                for name, table, col in (("u", eu, u_col), ("v", ev, v_col)):
                    for k in range(PK):
                        if name == "u" and k == UR // 2:
                            q.wait_ge(sems("blocks_used"), 23)
                        E.wait(name + "_slot_free")
                        E.hold()
                        s = k % UR
                        g.indirect_dma_start(ring_t[0:rows, col(s):col(s) + DM], None, table,
                                             bass.IndirectOffsetOnAxis(tok[0:rows, par * PK + k:par * PK + k + 1], 0)
                                             ).then_inc(sems(f"{name}{s}_in"), 16)

            q.wait_ge(sems("blocks_used"), 22)
            E.hold()
            for t in range(NT):
                with E.loop(TRIPS[t], seen__idx_ready=2, seen__u_slot_free=2 * PK, seen__v_slot_free=2 * PK):
                    head(t, P)
                    head(1 - t, P)
                if t == 0:
                    head(0, AH * NB)
            head(1, P)
            head(0, P)

        @block.tensor
        def _(q):
            E = Engine(q, sems, "pe")

            def mm(out, lhsT, rhs, start=True, stop=True):
                return nc.tensor.matmul(out, lhsT, rhs, start=start, stop=stop)

            def acc(out, lhsT, rhs):
                return nc.tensor.matmul(out, lhsT, rhs, start=False, stop=False, skip_group_check=True)

            def zero(out, rows, zeros):
                return nc.tensor.matmul(out, zeros[:, 0:rows], zeros, start=True, stop=False, skip_group_check=True)

            def tr(out, in_):
                rows = in_.shape[0]
                return nc.tensor.transpose(out, in_, cst[0:rows, C_EYE:C_EYE + rows])

            def block_in(n):
                q.wait_ge(sems(block_sem(n)[0]), block_sem(n)[1])

            def used():
                E.sync()
                q.sem_inc(sems("blocks_used"), 1)

            q.wait_ge(sems("consts_in"), 16)
            q.wait_ge(sems("c_in"), 32)
            for k in range(KT):
                m = tr(bank[7][:, 9 * k:9 * k + 9], RA[0:9, k * P:(k + 1) * P])
            E.op(m, "setup_mm")
            E.wait("setup_in")
            for n in range(12):
                block_in(n)
                if n >= 2:
                    E.wait("ada_out")
                for k in range(KT):
                    m = mm(bank[n % 2][0:9, :], silT[:, 9 * k:9 * k + 9], ring[:, SLOT[n], k * N:(k + 1) * N],
                           start=(k == 0), stop=(k == KT - 1))
                E.op(m, "ada_mm")
                used()
            E.wait("ada_out", 2)
            for k in range(16):
                m = tr(bank[7][:, 9 * k:9 * k + 9], MOD[0:9, k * P:(k + 1) * P])
            E.op(m, "setup_mm")
            q.wait_ge(sems("cw_in"), 80)
            for k in range(KT):
                m = tr(bank[6][:, 30 * k:30 * k + 30], RA[0:30, 1024 + k * P:1024 + (k + 1) * P])
            E.op(m, "setup_mm")
            q.wait_ge(sems("tab_in"), 32)
            E.op(mm(bank[5][0:AH, 0:RPITCH], tab[0:NBUCK + 1, :], RA[0:NBUCK + 1, 2048:2048 + RPITCH]), "setup_mm")
            E.wait("setup_in")
            mm(bank[4][:, 0:P], RA[0:NBUCK, 2560:2688], RA[0:NBUCK, 2048 + RPITCH:2048 + RPITCH + PG], stop=False)
            E.op(mm(bank[4][:, 0:P], RA[0:NBUCK, 2688:2816],
                    cst[0:NBUCK, NBUCK - 1:NBUCK].broadcast_to([NBUCK, P]), start=False), "setup_mm")

            for t in range(3):
                rows = P if t < 2 else NB
                E.wait("xhat_ready")
                if t >= 1:
                    E.wait("xT_out")
                for k in range(KT):
                    m = tr(bank[k // 4][:, (k % 4) * rows:(k % 4 + 1) * rows], H2[0:rows, t, k * P:(k + 1) * P])
                E.op(m, "xT")
            E.wait("xT_out")

            def q_rows(b):
                if b >= 2:
                    E.wait("q_rows_used")
                one = cst[0:NB, C_EYE + b:C_EYE + b + 1].broadcast_to([NB, P])
                E.op(mm(bank[4 + b % 2][:], one, SN[0:NB, 0:AW]), "q_rows")

            def logits_T(b):
                E.wait("k_logits")
                if b >= 2:
                    E.wait("lt_out")
                E.op(tr(bank[6 + b % 2][:, 0:P], LK[b % 2]), "lt_T")

            q.sem_inc(sems("lt_T"), 2)
            E.tally(("made", "lt_T")).n = 2
            job = [0]

            def proj_bank():
                job[0] += 1
                if job[0] > 4:
                    E.wait("proj_out")
                return bank[(job[0] - 1) % 4]

            def proj_done(m):
                E.op(m, "proj_mm")
                if job[0] in ROWS_AT:
                    b = ROWS_AT[job[0]]
                    q_rows(b)
                    logits_T(b - 2)

            for j in range(7):
                n = 12 + j
                block_in(n)
                if j in (0, 1, 3, 4):
                    for c in range(4):
                        b = proj_bank()
                        for k in range(KT):
                            m = mm(b[:, 0:R], ring[:, SLOT[n], k * N + c * P:k * N + (c + 1) * P], HTv[:, k, :],
                                   start=(k == 0), stop=(k == KT - 1))
                        proj_done(m)
                else:
                    for t in range(3):
                        b = proj_bank()
                        r0, rows = t * P, (P if t < 2 else NB)
                        for k in range(KT):
                            m = mm(b[0:rows, :], HTv[:, k, r0:r0 + rows], ring[:, SLOT[n], k * N:(k + 1) * N],
                                   start=(k == 0), stop=(k == KT - 1))
                        proj_done(m)
                used()
                if j == 0:
                    q.wait_ge(sems("proj_out"), 4)
                    for c in range(4):
                        m = tr(bank[7][0:NB, c * P:(c + 1) * P], QKT[:, c, SEQ:R])
                    E.op(m, "aq_T")
                    E.wait("aq_out")
                    q_rows(0)
                    q_rows(1)
            q.wait_ge(sems("wg_in"), 16)
            for t in range(3):
                b = proj_bank()
                r0, rows = t * P, (P if t < 2 else NB)
                for k in range(KT):
                    m = mm(b[0:rows, 0:8], HTv[:, k, r0:r0 + rows], WG8[:, k * 8:(k + 1) * 8], start=(k == 0), stop=(k == KT - 1))
                proj_done(m)
            E.wait("proj_out", 4)

            for t in range(2):
                for c in range(4):
                    m = tr(bank[t][:, c * P:(c + 1) * P], QKT[:, 4 + c, t * P:(t + 1) * P])
                E.op(m, "nat_T")
            for c in range(4):
                m = tr(bank[2][0:NB, c * P:(c + 1) * P], QKT[:, 4 + c, SEQ:R])
            E.op(m, "nat_T")
            E.wait("nat_out", 3)
            for c in range(8):
                m = tr(bank[c // 4][0:11, (c % 4) * P:(c % 4 + 1) * P], QKT[:, 8 + c, SEQ - 3:R])
            E.op(m, "nat_T")
            E.wait("nat_out")
            for b in (6, 7):
                logits_T(b)
            E.wait("lt_out", 2)
            E.wait("gate_in")
            tr(bank[4][0:NB, 0:P], gs)
            E.op(tr(bank[4][0:NB, P:2 * P], rmx), "gate_mm")
            E.wait("gate_in")
            E.op(tr(bank[4][:, 256:256 + NB], RA[0:NB, 5000:5128]), "gate_mm")
            for b in range(NB):
                E.wait("exp_b")
                if b >= 2:
                    E.wait("pT_out")
                E.op(tr(bank[5 + b % 2][:, 0:P], LTv[:, b, :]), "pT")
            E.wait("pT_out", 2)
            E.op(tr(bank[4][0:NB, 0:P], rs), "gate_mm")
            q.wait_ge(sems("rs_seen"), 1)
            for n in (7, 4):
                nc.tensor.matmul(bank[n][:], cst[0:NB, C_LOW:C_LOW + 1].broadcast_to([NB, P]), cst[0:NB, 0:N],
                                 start=True, stop=False, skip_group_check=True)
            E.tally(("made", "kv_used")).n = 18
            vh = [0]

            def values(count=1):
                for _ in range(count):
                    b, hf = vh[0] // 2, vh[0] % 2
                    q.wait_ge(sems(f"kv{hf}"), 128 * (NB + b + 1))
                    for g in range(8):
                        pg = hf * 8 + g
                        m = acc(bank[7 if b < 4 else 4][32 * (b % 4):32 * (b % 4) + AH, :], LTv[:, b, pg * 8:pg * 8 + 8],
                                ring[:, 2 + hf, g * N:(g + 1) * N])
                    E.op(m, "kv_used")
                    vh[0] += 1

            L = RA[:, 2048:4096].rearrange("p (h n) -> p h n", h=AH)
            PT = RA[:, 4096:6144].rearrange("p (h n) -> p h n", h=AH)
            for t in range(NT):
                w = P * (t + 1)
                for h2 in range(4):
                    if h2 + 4 * t >= 2:
                        E.wait("logits_used")
                    for e in range(2):
                        hp = slice(64 * e, 64 * e + 64)
                        m = mm(bank[LB[2 * (h2 % 2) + e]][:, 0:w], QKT[hp, h2, t * P:(t + 1) * P], QKT[hp, 4 + h2, 0:w])
                    E.op(m, "logits")
                values()
                E.wait("probs")
                for s in range(t + 1):
                    for hh in range(2):
                        if (t, s, hh) != (0, 0, 0):
                            E.wait("probsT_out")
                        for e in range(4):
                            m = tr(bank[2][:, e * P:(e + 1) * P], L[:, 4 * hh + e, s * P:(s + 1) * P])
                        E.op(m, "probsT")
                values()
                E.wait("probsT_out")
                if t:
                    E.wait("attn_out")
                for h in range(AH):
                    for s in range(t + 1):
                        m = mm(bank[3][:, h * AD:(h + 1) * AD], PT[:, h, s * P:(s + 1) * P],
                               NAT[:, s, h * AD:(h + 1) * AD], start=(s == 0), stop=(s == t))
                E.op(m, "attn_mm")
                if t == 0:
                    E.tally(("seen", "probsT_out")).n -= 1
            E.wait("logits_used", 2)
            E.wait("attn_out")

            E.wait("logf_ready")
            E.op(mm(bank[0][:, 0:12], upto, g_lf), "cum")
            E.wait("conv_ready")
            for c in range(2):
                cs = slice(c * P, (c + 1) * P)
                for h in range(MH):
                    m = tr(bank[1][:, h * P:(h + 1) * P], QK[:, MH + h, cs])
                E.op(m, "kn_T")
                for h in range(MH):
                    m = mm(bank[2][:, h * P:(h + 1) * P], QK[:, MH + h, cs], QK[:, h, cs])
                E.op(m, "kq")
                values()
                E.wait("diag_a")
                E.op(mm(bank[3][:], ones, RA[:, 4608:5120]), "a_rows")
                values()
                E.wait("mm_diag")
                E.op(mm(bank[3][:], ones, RA[:, 4608:5120]), "m_rows")
                E.op(mm(bank[0][:, 16:24], cst[:, C_EYE + P - 1:C_EYE + P].broadcast_to([P, P]), bc8), "last_row")
                if c == 1:
                    for h in range(MH):
                        mm(bank[5][:, h * P:(h + 1) * P], QK[:, h, cs], CT[:, h, :])
                values()
                E.wait("st_ready")
                for h in range(MH):
                    mm(bank[6][:, h * P:(h + 1) * P], ST[:, h, :], NAT[:, c, N + h * P:N + (h + 1) * P])
                if c == 1:
                    for h in range(MH):
                        mm(bank[0][:, 28 + h:29 + h], QK[:, h, cs], nst[:, h:h + 1])
                for h in range(MH):
                    m = mm(bank[0][:, 24 + h:25 + h], ST[:, h, :], ones[:, 0:1])
                E.op(m, "intra")
                E.wait("wv_ready")
                E.wait("kn_out")
                for h in range(MH):
                    mm(bank[1][:, h * P:(h + 1) * P], KN[:, h, :], WV[:, h, :])
                for h in range(MH):
                    m = mm(bank[2][:, h:h + 1], KN[:, h, :], ex[:, 8 + h:9 + h])
                E.op(m, "state_mm")
                values()
                E.wait("chunk_done")
            for h in range(MH):
                tr(bank[1][:, h * P:(h + 1) * P], CT[:, h, :])
            E.op(tr(bank[2][0:MH, 0:P], nst), "state_T")
            E.wait("state_T_out")

            values()
            for c in range(8):
                m = tr(bank[2 + c // 4][0:NB, (c % 4) * P:(c % 4 + 1) * P], YS[:, (c + 4) % 8, :])
            E.op(m, "kqn_T")
            E.wait("smem_in")
            E.op(mm(bank[5][:, 0:32], ones8, KQW), "smem_mm")
            E.wait("smem_in")
            for h in range(MH):
                m = tr(bank[6][:, h * 8:(h + 1) * 8], EV[:, h * P:(h + 1) * P])
            E.op(m, "smem_mm")
            def mix_T(t, b0):
                rows = P if t < 2 else NB
                for k in range(KT):
                    m = tr(bank[b0 + k // 4][:, (k % 4) * rows:(k % 4 + 1) * rows], MIXv[0:rows, t, k * P:(k + 1) * P])
                E.op(m, "tail_mm")
                E.wait("mixT_out")

            mix_T(0, 0)
            mix_T(1, 0)
            E.wait("kqn_out")
            E.wait("ev_out")
            E.wait("w2_zero")

            def kq_rows(b):
                if b >= 2:
                    E.wait("kq_used")
                one_b = cst[:, C_EYE + b:C_EYE + b + 1].broadcast_to([P, P])
                mm(bank[KQ_BANKS[b % 2][0]][:], one_b, W2[:, 0:N])
                E.op(mm(bank[KQ_BANKS[b % 2][1]][:], one_b, W2[:, N:2 * N]), "kq_rows")

            def y_rows(t, j, between=None):
                for k in range(KT):
                    if between is not None:
                        between(k)
                    m = mm(bank[2 * j + t][:], HTv[:, k, t * P:(t + 1) * P], ring[:, SLOT[BO + j], k * N:(k + 1) * N],
                           start=(k == 0), stop=(k == KT - 1))
                return m

            def smem_and_values(j):
                def between(k):
                    if k % 2 == 0:
                        kq_rows(4 * j + k // 2)
                    if k % 4 == 3 and vh[0] < 16:
                        values()
                return between

            for j in range(2):
                block_in(BO + j)
                m = y_rows(0, j, smem_and_values(j))
            E.op(m, "y_mm")
            E.wait("c_new")
            for h in range(MH):
                m = tr(bank[5][0:NB, h * P:(h + 1) * P], numS[:, h * 8:(h + 1) * 8])
            E.op(m, "smem_mm")
            E.wait("vo_ready")
            for e in range(2):
                m = mm(bank[6][0:NB, :], cst[:, C_SUM + 8 * e:C_SUM + 8 * e + 8], VO[:, e, :],
                       start=(e == 0), stop=(e == 1))
            E.op(m, "gate_mm")
            for j in range(2):
                m = y_rows(1, j)
            E.op(m, "y_mm")
            E.wait("smem_done")
            mix_T(2, 4)
            for j in range(2):
                n = BO + j
                for k in range(KT):
                    m = mm(bank[6 + j][0:NB, :], HTv[:, k, SEQ:R], ring[:, SLOT[n], k * N:(k + 1) * N],
                           start=(k == 0), stop=(k == KT - 1))
                E.op(m, "y_mm")
                used()
            for t in range(3):
                rows = P if t < 2 else NB
                E.wait("h2_ready")
                for k in range(KT):
                    m = tr(bank[4 + k // 4][:, (k % 4) * rows:(k % 4 + 1) * rows], H2[0:rows, t, k * P:(k + 1) * P])
                E.op(m, "tail_mm")
                E.wait("h2T_out")
            q.wait_ge(sems("sk_in"), 16)
            for e in range(2):
                m = tr(bank[3][:, e * P:(e + 1) * P], SKN[:, e * P:(e + 1) * P])
            E.op(m, "tail_mm")
            E.tally(("made", "scores")).n = 1

            def scores():
                E.wait("qs_ready")
                E.wait("scores_used")
                for e in range(2):
                    m = mm(bank[0][:, e * P:(e + 1) * P], QS[:, e * P:(e + 1) * P], SKT[:, e * P:(e + 1) * P])
                E.op(m, "scores")

            for c in range(16):
                n = BQ + (c // 4 + 2) % 4
                if c % 4 == 0:
                    block_in(n)
                if c >= 4:
                    E.wait("q_out")
                for k in range(KT):
                    m = mm(bank[4 + c % 4][:, 0:R], ring[:, SLOT[n], k * N + (c % 4) * P:k * N + (c % 4 + 1) * P], HTv[:, k, :],
                           start=(k == 0), stop=(k == KT - 1))
                E.op(m, "tail_mm")
                if c == 2:
                    scores()
                if c % 4 == 3:
                    used()
                    if c >= 8:
                        q.sem_inc(sems("v_slot_free"), UR // 2)
            E.wait("q_out", 4)
            for e in range(2):
                m = mm(bank[1 + e][0:64, :], cst[0:NB, C_REP:C_REP + 64], H2[0:NB, 2, e * N:(e + 1) * N])
            E.op(m, "tail_mm")
            E.wait("h2r_out")
            E.wait("sk_out")

            E.wait("zeros_ready")
            E.tally(("made", "v_slot_free")).n = UR
            E.tally(("seen", "diag_w")).n = 2 * PK

            def head(rows, fb, base, i=None):
                out_rows = P if rows == P else NB
                for k in range(PK):
                    s = k % UR
                    count = 16 * (base + k // UR + 1)
                    q.wait_ge(sems(f"v{s}_in"), count if i is None else i * 64 + count)
                    E.wait("diag_w")
                    for e in range(2):
                        m = acc(bank[fb + e][0:out_rows, :], MIX[0:rows, (k % 4) * P:(k % 4) * P + out_rows],
                                ring_t[0:rows, v_col(s) + e * N:v_col(s) + (e + 1) * N])
                    E.op(m, "v_slot_free")

            for t in range(NT):
                fb = 4 + 2 * t
                zero(bank[fb][:], P, MIX[0:NB, 2048:2560])
                zero(bank[fb + 1][:], P, MIX[0:NB, 2048:2560])
                with E.loop(TRIPS[t], seen__qs_ready=2, seen__scores_used=2, made__scores=2, seen__diag_w=2 * PK,
                            made__v_slot_free=2 * PK) as i:
                    for e in range(2):
                        scores()
                        head(P, fb, BASE[t] + 2 * e, i)
                if t == 1:
                    scores()
                    head(P, fb, BASE[t] + 4 * TRIPS[t])
                    head(P, fb, BASE[t] + 4 * TRIPS[t] + 2)
                E.sync()
                q.sem_inc(sems("f_ready"), 1)
                if t == 0:
                    zero(bank[2][0:NB, :], NB, MIX[0:NB, 2048:2560])
                    zero(bank[3][0:NB, :], NB, MIX[0:NB, 2048:2560])
                    scores()
                    head(AH * NB, 2, 2 * PH)
                    E.sync()
                    q.sem_inc(sems("f_ready"), 1)

        @block.scalar
        def _(q):
            E = Engine(q, sems, "act")
            a = nc.scalar
            stores = [0]

            def store(dst, src, name="stored"):
                q.dma_start(dst, src).then_inc(sems(name), 16)
                stores[0] += 16 * (name == "stored")

            def sigmoid(pairs, name):
                for dst, src in pairs:
                    E.op(a.activation(dst, src, ACT.Exp, scale=-1.0))
                E.sync()
                for dst, src in pairs:
                    E.op(a.activation(dst, dst, ACT.Ln, bias=1.0))
                E.sync()
                for k, (dst, src) in enumerate(pairs):
                    E.op(a.activation(dst, dst, ACT.Exp, scale=-1.0), name if k == len(pairs) - 1 else None)

            E.wait("setup_mm")
            E.op(a.activation(silT, bank[7][:, 0:72], ACT.Exp, scale=-1.0), "pre_exp")
            E.wait("mods_T")
            q.dma_start(mods, MOD[8:9, :]).then_inc(sems("mods_out"), 16)
            for t in range(2):
                E.wait("xT")
                for k in range(KT):
                    m = a.activation(HTv[:, k, t * P:(t + 1) * P], bank[k // 4][:, (k % 4) * P:(k % 4 + 1) * P],
                                     ACT.Identity, scale=scT1[:, 9 * k + 8:9 * k + 9], bias=shT[:, 9 * k + 8:9 * k + 9])
                E.op(m, "xT_out")
            job = [0]

            def out(dst, rows, cols):
                E.wait("proj_mm")
                E.op(a.activation(dst, bank[job[0] % 4][0:rows, 0:cols], ACT.Copy), "proj_out")
                job[0] += 1
                if job[0] in ROWS_AT:
                    logits_T()

            def logits_T():
                b = rows_out[0]
                rows_out[0] += 1
                E.wait("lt_T")
                E.op(a.activation(LTv[:, b, :], bank[6 + b % 2][:, 0:P], ACT.Copy, scale=SC_A, accum_out=gs[:, b:b + 1]), "lt_out")

            rows_out = [0]
            E.tally(("seen", "lt_T")).n = 2
            w_in = A["w_in"].rearrange("o (k p) n -> (o p) k n", p=P)
            w_o = A["w_out"].rearrange("o (k p) n -> (o p) k n", p=P)

            def weights(n, w, j):
                q.wait_ge(sems("blocks_used"), n - 1)
                q.dma_start(ring[:, SLOT[n], :].rearrange("p (k n) -> p k n", k=KT),
                            w[:, :, j * N:(j + 1) * N]).then_inc(sems(block_sem(n)[0]), 16)

            for j, dst in enumerate((0, 4, None, 8, 12, None, None)):
                if dst is not None:
                    for c in range(4):
                        out(QKT[:, dst + c, :], P, R)
                else:
                    o = {2: 0, 5: 1, 6: 2}[j]
                    for t in range(2):
                        out(NAT[:, t, o * N:(o + 1) * N], P, N)
                    out(SN[0:NB, 1024 + o * N:1024 + (o + 1) * N], NB, N)
                if j < 5:
                    weights(14 + j, w_in, j + 2)
                elif j == 5:
                    weights(BO, w_o, 0)
                if j == 0:
                    E.wait("aq_T")
                    E.op(a.activation(SN[0:NB, 0:N], bank[7][0:NB, :], ACT.Copy), "aq_out")
            E.wait("g_zero")
            for t in range(3):
                out(G3[0:P if t < 2 else NB, t, :], P if t < 2 else NB, 8)
            for t in range(2):
                E.wait("nat_T")
                E.op(a.activation(MIX[:, t * N:(t + 1) * N], bank[t][:], ACT.Copy), "nat_out")
            E.wait("nat_T")
            E.op(a.activation(SN[0:NB, N:2 * N], bank[2][0:NB, :], ACT.Copy), "nat_out")
            E.wait("nat_T")
            for e in range(2):
                E.op(a.activation(MIX[0:11, 1024 + e * N:1024 + (e + 1) * N], bank[e][0:11, :], ACT.Copy), "nat_out" if e else None)
            for b in (6, 7):
                logits_T()
            E.sync()
            kp, vp = (O[n].rearrange("o b s h d -> (o b s) (h d)") for n in ("k_prompt", "v_prompt"))
            ks, vs = (O[n].rearrange("o b s h d -> (o b s) (h d)") for n in ("k_sample", "v_sample"))
            store(kp.rearrange("(t p) n -> p t n", p=P), MIX[:, 0:1024].rearrange("p (t n) -> p t n", t=2))
            store(vp.rearrange("(t p) n -> p t n", p=P), NAT[:, :, 0:N])
            store(ks, SN[0:NB, N:2 * N])
            store(vs, SN[0:NB, 2 * N:3 * N])
            store(O["conv_prompt"].rearrange("o b j c -> (o b j) c"), MIX[0:3, 1024:2048])
            store(O["conv_sample"].rearrange("o b j c -> (o b) j c")[:, 2, :], MIX[3:11, 1024:2048])
            store(O["conv_sample"].rearrange("o b j c -> (o b) j c")[:, 0:2, :],
                  A["state_conv"].rearrange("o b j c -> (o b) j c")[:, 1:3, :])
            E.wait("gate_arg")
            E.op(a.activation(g_ab, g_ab, ACT.Exp, scale=-1.0))
            E.sync()
            E.op(a.activation(g_ab, g_ab, ACT.Ln, bias=1.0), "ln_ready")
            E.wait("nbT_ready")
            E.op(a.activation(pn[0:NB, :], pn[0:NB, :], ACT.Exp), "pn_ready")
            for b in range(NB + 1):
                if b < NB:
                    E.op(a.activation(LTv[:, b, :], LTv[:, b, :], ACT.Exp, bias=nbT[:, b:b + 1], accum_out=rs[:, b:b + 1]), "exp_b")
                if b:
                    E.wait("pT")
                    E.op(a.activation(LTv[:, b - 1, :], bank[5 + (b - 1) % 2][:, 0:P], ACT.Copy), "pT_out")
            q.wait_ge(sems("stored"), stores[0])
            q.sem_inc(sems("rows_stored"), 1)

            L = RA[:, 2048:4096].rearrange("p (h n) -> p h n", h=AH)
            for t in range(NT):
                E.wait("row_max")
                for h in range(AH):
                    m = a.activation(L[:, h, 0:P * (t + 1)], L[:, h, 0:P * (t + 1)], ACT.Exp, bias=a_mx[:, h:h + 1],
                                     accum_out=a_sum[:, h:h + 1])
                E.op(m, "probs")
                if t == 0:
                    E.wait("conv_arg")
                    sigmoid([(E8, QK), (YT, YS)], "sigm_ready")
                    q.wait_ge(sems("conv_ready"), 1)
                    weights(BO + 1, w_o, 1)
            sigmoid([(MIXv[:, 0:2, N:2 * N], NAT[:, :, 2 * N:3 * N]), (MIX[0:NB, 2560:3072], SN[0:NB, 2048:2560])], "og_ready")
            for c in range(2):
                E.wait("kn_T")
                E.op(a.activation(RA[:, 2048:2560], bank[1][:], ACT.Copy), "kn_out")
                E.wait("ex_args")
                E.op(a.activation(ex, ex, ACT.Exp), "ex_ready")
                for h in range(MH):
                    m = a.activation(WT[:, h, :], WT[:, h, :], ACT.Exp, bias=g_a[:, 4 * c + h:4 * c + h + 1])
                E.op(m, "wt_ready")
            E.wait("state_T")
            E.op(a.activation(RA[:, 4096:4608], bank[1][:], ACT.Copy))
            E.op(a.activation(RA[0:MH, 4608:4736], bank[2][0:MH, 0:P], ACT.Copy), "state_T_out")
            E.sync()
            store(O["C_prompt"].rearrange("o b h v k -> v (o b h) k"), WV)
            store(O["n_prompt"].rearrange("o b h k -> (o b h) k"), RA[0:MH, 4608:4736])
            store(O["m_prompt"].rearrange("o b h -> (o b) h"), mprev[0:1, :])
            q.wait_ge(sems("stored"), stores[0])
            q.dma_start(CS.rearrange("p b h k -> p (b h) k"), A["state_C"].rearrange("o b h v k -> v (o b h) k")).then_inc(sems("cs_in"), 16)
            q.dma_start(NS.rearrange("b (h k) -> b h k", h=MH), A["state_n"].rearrange("o b h k -> (o b) h k")).then_inc(sems("ns_in"), 16)
            E.wait("kqn_T")
            E.op(a.activation(KQN[:, 0:N], bank[2][0:NB, :], ACT.Copy))
            E.op(a.activation(KQN[:, N:2 * N], bank[3][0:NB, :], ACT.Copy), "kqn_out")
            E.wait("sE_args")
            E.op(a.activation(sE[0:NB, :], sE[0:NB, :], ACT.Exp), "sE_ready")
            for t in range(3):
                r0, rows = t * P, (P if t < 2 else NB)
                b0 = 0
                if t == 2:
                    b0 = 4
                    E.wait("c_new")
                    store(O["C_sample"].rearrange("o b h v k -> v (o b h) k"), CS.rearrange("p b h k -> p (b h) k"), "cs_stored")
                    store(O["n_sample"].rearrange("o b h k -> (o b) h k"), NS.rearrange("b (h k) -> b h k", h=MH))
                    store(O["m_sample"].rearrange("o b h -> (o b) h"), sM[0:NB, :])
                E.wait("tail_mm")
                for k in range(KT):
                    m = a.activation(HTv[:, k, r0:r0 + rows], bank[b0 + k // 4][:, (k % 4) * rows:(k % 4 + 1) * rows],
                                     ACT.Copy, scale=cwT[:, 30 * k + 5:30 * k + 6])
                E.op(m, "mixT_out")
            for t in range(3):
                r0, rows = t * P, (P if t < 2 else NB)
                E.wait("tail_mm")
                for e in range(2):
                    m = a.activation(HTv[:, 4 * e:4 * e + 4, r0:r0 + rows],
                                     bank[4 + e][:, 0:4 * rows].rearrange("p (k r) -> p k r", k=4), ACT.Copy)
                    if e == 0:
                        E.op(m)
                E.op(m, "h2T_out")
            E.wait("tail_mm")
            E.op(a.activation(SKT, bank[3][:, 0:256], ACT.Copy), "sk_out")
            E.wait("qt_zero")
            QTf = R1[:, 3 * DM:3 * DM + 17 * 256]

            def next_query(off):
                E.wait("scores")
                E.op(a.activation(QS, QTf[:, off], ACT.Copy), "qs_ready")

            def best(par):
                E.wait("best_ready")
                E.op(a.activation(ebs[par], bs[par], ACT.Exp, bias=nbs[par], accum_out=esum[par]), "best_exp")

            for c in range(16):
                E.wait("tail_mm")
                h, e = c // 2, c % 2
                E.op(a.activation(QT[:, h:h + PH + 2:PH + 1, e, :], bank[4 + c % 4][:, 0:SEQ].rearrange("p (t r) -> p t r", t=2), ACT.Copy))
                E.op(a.activation(QT[:, PH, e, h * NB:(h + 1) * NB], bank[4 + c % 4][:, SEQ:R], ACT.Copy), "q_out")
                if c == 1:
                    E.sync()
                    q.sem_inc(sems("scores"), 1)
                    next_query(slice(0, 256))
                if c == 7:
                    best(0)
            E.wait("tail_mm")
            q.wait_ge(sems("cs_stored"), 16)
            for e in range(2):
                E.op(a.activation(RA[0:64, 5120 + e * N:5120 + (e + 1) * N], bank[1 + e][0:64, :], ACT.Copy),
                     "h2r_out" if e else None)

            E.tally(("seen", "v_slot_free")).n = UR - 4
            E.tally(("made", "diag_w")).n = 2 * PK

            def head(par, rows, nxt=None):
                if nxt is not None:
                    next_query(nxt)
                E.wait("gelu_arg")
                E.op(a.activation(wB[0:rows, :], wB[0:rows, :], ACT.Exp), "gelu_exp")
                E.wait("w_ready")
                out_rows = P if rows == P else NB
                src = eye if rows == P else cst[0:rows, C_HS:C_HS + NB]
                for k in range(PK):
                    E.wait("v_slot_free")
                    E.op(a.activation(MIX[0:rows, (k % 4) * P:(k % 4) * P + out_rows], src, ACT.Copy,
                                      scale=wG[par][0:rows, k:k + 1]), "diag_w")
                if nxt is not None:
                    best(1 - par)

            def finish(t):
                rows = P if t < 2 else NB
                E.wait("var2_ready")
                E.op(a.activation(rstd[0:rows, t:t + 1], mv[0:rows, 2 * t + 1:2 * t + 2], ACT.Ln))
                E.sync()
                E.op(a.activation(rstd[0:rows, t:t + 1], rstd[0:rows, t:t + 1], ACT.Exp, scale=-0.5), "rstd2_ready")
                E.wait("y_ready")
                if t < 2:
                    store(O["y_prompt"].rearrange("o (t p) d -> (o p) t d", p=P)[:, t, :], Xv[:, t, :])
                else:
                    store(O["y_sample"].rearrange("b o d -> (b o) d"), Xv[0:NB, 2, :])

            q.wait_ge(sems("stored"), stores[0])
            for t in range(NT):
                first = t * (PH + 1)
                with E.loop(TRIPS[t], seen__scores=2, made__qs_ready=2, seen__gelu_arg=2, made__gelu_exp=2, seen__w_ready=2,
                            seen__v_slot_free=2 * PK, made__diag_w=2 * PK, seen__best_ready=2, made__best_exp=2) as i:
                    for e in range(2):
                        head(e ^ t, P, bass.ds(i * 512 + (first + e + 1) * 256, 256))
                if t == 0:
                    head(0, AH * NB, slice((PH + 1) * 256, (PH + 2) * 256))
                    finish(0)
            finish(2)
            head(1, P, slice(2 * PH * 256, (2 * PH + 1) * 256))
            head(0, P)
            finish(1)
            q.wait_ge(sems("stored"), stores[0])

        @block.vector
        def _(q):
            E = Engine(q, sems, "dve")
            v = nc.vector

            def step(ins, name=None):
                E.op(ins, name)
                E.sync()

            q.sem_inc(sems("kv_used"), 2)
            E.op(v.memset(G, 0.0), "g_zero")
            E.op(v.memset(tab[NBUCK:NBUCK + 1, :], NEG))
            E.wait("pre_exp")
            E.wait("setup_mm")
            step(v.tensor_scalar(silT, silT, 1.0, None, ALU.add))
            step(v.reciprocal(silT, silT))
            E.op(v.tensor_tensor(silT, silT, bank[7][:, 0:72], ALU.mult), "setup_in")
            q.wait_ge(sems("tab_in"), 32)
            step(v.memset(RA[0:NBUCK, 2560:2816], 0.0))
            E.op(v.tensor_copy(RA[0:NBUCK, 2560 + 120:2688], tab[0:NBUCK, :]))
            E.op(v.tensor_copy(RA[0:NBUCK, 2688:2808].rearrange("p (g h) -> p g h", g=15),
                               tab[0:NBUCK, :].unsqueeze(1).broadcast_to([NBUCK, 15, AH])), "setup_in")
            q.wait_ge(sems("x_in"), 32)
            for t in range(3):
                rows = P if t < 2 else NB
                norm_rows(E, t, Xv[0:rows, t, :], rows, H2[0:rows, t, :], "xhat_ready")
            q.wait_ge(sems("bada_in"), 16)
            for n in range(12):
                E.wait("ada_mm")
                E.op(v.tensor_tensor(MOD[0:9, n * N:(n + 1) * N], bank[n % 2][0:9, :], MOD[0:9, n * N:(n + 1) * N], ALU.add), "ada_out")
            E.wait("setup_mm")
            E.op(v.tensor_copy(shT, bank[7][:, 0:72]))
            E.op(v.tensor_scalar(scT1, bank[7][:, 72:144], 1.0, None, ALU.add), "mods_T")
            E.wait("setup_mm")
            E.op(v.tensor_copy(cwT, bank[6][:, 0:240]), "cwT_ready")
            E.wait("setup_mm")
            E.op(v.tensor_copy(RA[0:AH, 4096:4096 + RPITCH], bank[5][0:AH, 0:RPITCH]), "rel_ready")
            E.wait("setup_mm")
            E.op(v.tensor_copy(BT, bank[4][:, 0:P]))
            E.wait("xT", 3)
            E.sync()
            sc3 = scT1.rearrange("p (k n) -> p k n", k=KT)
            sh3 = shT.rearrange("p (k n) -> p k n", k=KT)
            for e in range(2):
                ks = slice(4 * e, 4 * e + 4)
                E.op(v.tensor_tensor(HTv[:, ks, SEQ:R], bank[e][:, 0:32].rearrange("p (k b) -> p k b", k=4), sc3[:, ks, 0:NB], ALU.mult))
            E.sync()
            E.op(v.tensor_tensor(HTv[:, :, SEQ:R], HTv[:, :, SEQ:R], sh3[:, :, 0:NB], ALU.add), "xT_out")

            E.tally(("made", "kv_used")).n = 2
            KP = RA[:, 2048:6144].rearrange("p (g n) -> p g n", g=8)
            q.wait_ge(sems("rel_out"), 16)
            with E.loop(4, seen__q_rows=2, made__k_logits=2, made__kv_used=4, seen__lt_T=2, made__dve_steps=2) as i:
                for e in range(2):
                    E.wait("q_rows")
                    E.wait("lt_T")
                    for hf in range(2):
                        slot = ring[:, 2 + hf, :].rearrange("p (g n) -> p g n", g=8)
                        q.wait_ge(sems(f"kv{hf}"), i * 256 + (e * 128 + 128))
                        E.op(v.tensor_tensor(KP, slot, bank[4 + e][:].unsqueeze(1).broadcast_to([P, 8, AW]), ALU.mult), "kv_used")
                        E.sync()
                        if hf:
                            q.sem_inc(sems("q_rows_used"), 1)
                        E.op(v.tensor_reduce(LK[e][:, hf * 64:(hf + 1) * 64], KP.rearrange("p g (h d) -> p (g h) d", h=AH),
                                             AX, ALU.add), "k_logits" if hf else None)
                        E.sync()
            q.wait_ge(sems("smst_in"), 32)
            E.wait("nat_out", 3)
            tmp = RA[0:NB, 4608:5120]
            step(v.tensor_tensor(tmp, SN[0:NB, 0:AW], SN[0:NB, AW:2 * AW], ALU.mult))
            step(v.tensor_reduce(nl[0:NB, :], tmp.rearrange("p (h d) -> p h d", h=AH), AX, ALU.add))
            step(v.scalar_tensor_tensor(nl[0:NB, :], nl[0:NB, :], SC_A, smst[0:NB, 0:8], ALU.mult, ALU.add))
            q.wait_ge(sems("bgate_in"), 16)
            q.wait_ge(sems("proj_out"), 28)
            f3 = lambda x: x.rearrange("p (t n) -> p t n", t=3)
            step(v.tensor_tensor(G3, G3, bg.unsqueeze(1).broadcast_to([P, 3, 8]), ALU.add))
            E.op(v.scalar_tensor_tensor(f3(g_ab), G3[:, :, 4:8], -1.0, G3[:, :, 4:8], ALU.mult, ALU.max), "gate_arg")
            E.op(v.tensor_scalar(f3(g_lf), G3[:, :, 4:8], 0.0, None, ALU.min))
            E.wait("lt_out", 8)
            step(v.tensor_tensor(LTv, LTv, BT.unsqueeze(1).broadcast_to([P, NB, P]), ALU.add))
            step(v.tensor_reduce(rmx, LTv, AX, ALU.max), "gate_in")
            E.wait("gate_mm")
            W = RA[0:NB, 2048:4096]
            g128, gate, c1, c2 = W[:, 0:128], W[:, 128:192], W[:, 512:1024], W[:, 1024:1536]
            rank, am, AM, rm = W[:, 192:256], W[:, 256:320], W[:, 320:448], W[:, 1536:1664]
            NBB = RA[0:NB, 5000:5128]
            step(v.tensor_copy(g128, bank[4][0:NB, 0:P]))
            pages = g128.rearrange("p (n two h) -> p h n two", two=2, h=AH)
            step(v.tensor_tensor(gate.rearrange("p (h n) -> p h n", h=AH), pages[:, :, :, 0], pages[:, :, :, 1], ALU.add))
            gm = gate.rearrange("p (h m) -> p h m", h=AH).unsqueeze(2).broadcast_to([NB, AH, NBLK, NBLK])
            gn = gate.rearrange("p (h n) -> p h n", h=AH).unsqueeze(3).broadcast_to([NB, AH, NBLK, NBLK])
            c14, c24 = (x.rearrange("p (h n m) -> p h n m", h=AH, n=NBLK) for x in (c1, c2))
            low = cst[0:NB, C_LOW:C_LOW + 64].rearrange("p (n m) -> p n m", n=NBLK).unsqueeze(1).broadcast_to([NB, AH, NBLK, NBLK])
            E.op(v.tensor_tensor(c14, gm, gn, ALU.is_gt))
            step(v.tensor_tensor(c24, gm, gn, ALU.is_equal))
            step(v.tensor_tensor(c24, c24, low, ALU.mult))
            step(v.tensor_tensor(c1, c1, c2, ALU.add))
            step(v.tensor_reduce(rank, c1.rearrange("p (x m) -> p x m", m=NBLK), AX, ALU.add))
            step(v.tensor_scalar(am, rank, TOPB - 0.5, NEG, ALU.is_gt, ALU.mult))
            E.op(v.tensor_copy(AM.rearrange("p (n two h) -> p n two h", two=2, h=AH),
                               am.rearrange("p (h n) -> p n h", h=AH).unsqueeze(2).broadcast_to([NB, NBLK, 2, AH])))
            E.sync()
            step(v.tensor_tensor(rm, bank[4][0:NB, P:2 * P], AM, ALU.add))
            step(v.tensor_reduce(m8[0:NB, :], rm.rearrange("p (g h) -> p h g", h=AH), AX, ALU.max))
            step(v.tensor_tensor(m8[0:NB, :], m8[0:NB, :], nl[0:NB, :], ALU.max))
            E.op(v.tensor_tensor(pn[0:NB, :], nl[0:NB, :], m8[0:NB, :], ALU.subtract))
            E.op(v.tensor_tensor(NBB.rearrange("p (g h) -> p g h", h=AH), AM.rearrange("p (g h) -> p g h", h=AH),
                                 m8[0:NB, :].unsqueeze(1).broadcast_to([NB, NPG, AH]), ALU.subtract), "gate_in")
            E.wait("gate_mm")
            step(v.tensor_copy(nbT, bank[4][:, 256:256 + NB]), "nbT_ready")
            E.wait("pn_ready")
            E.wait("gate_mm")
            step(v.tensor_reduce(ri8[0:NB, :], bank[4][0:NB, 0:P].rearrange("p (g h) -> p h g", h=AH), AX, ALU.add), "rs_seen")

            q.wait_ge(sems("rel_in"), 16)
            E.wait("rows_stored")
            B = RA[:, 0:2048].rearrange("p (h n) -> p h n", h=AH)
            L = RA[:, 2048:4096].rearrange("p (h n) -> p h n", h=AH)
            PT = RA[:, 4096:6144].rearrange("p (h n) -> p h n", h=AH)
            for t in range(NT):
                w = P * (t + 1)
                for h2 in range(4):
                    E.wait("logits")
                    for e in range(2):
                        E.op(v.scalar_tensor_tensor(L[:, 2 * h2 + e, 0:w], bank[LB[2 * (h2 % 2) + e]][:, 0:w], SC_A,
                                                    B[:, 2 * h2 + e, 2 * P - w:2 * P], ALU.mult, ALU.add),
                             "logits_used" if e else None)
                E.sync()
                E.op(v.tensor_reduce(a_mx, L[:, :, 0:w], AX, ALU.max, negate=True), "row_max")
                E.wait("probs")
                E.op(v.reciprocal(a_ri, a_sum))
                if t == 0:
                    q.wait_ge(sems("rel_out"), 16)
                for s in range(t + 1):
                    for hh in range(2):
                        E.wait("probsT")
                        E.op(v.tensor_copy(PT[:, 4 * hh:4 * hh + 4, s * P:(s + 1) * P],
                                           bank[2][:].rearrange("p (e n) -> p e n", e=4)), "probsT_out")
                E.wait("attn_mm")
                E.op(v.tensor_tensor(MIXv[:, t, 0:AW].rearrange("p (h d) -> p h d", h=AH),
                                     bank[3][:].rearrange("p (h d) -> p h d", h=AH),
                                     a_ri.unsqueeze(2).broadcast_to([P, AH, AD]), ALU.mult), "attn_out")
                E.sync()

            E.op(v.memset(ones, 1.0))
            E.wait("ln_ready")
            E.op(v.tensor_tensor(g_lf, g_lf, g_ab, ALU.subtract), "logf_ready")
            E.wait("cum")
            step(v.tensor_copy(g_b, bank[0][:, 0:12]))
            step(v.tensor_tensor(f3(g_a), G3[:, :, 0:4], f3(g_b), ALU.subtract))
            step(v.memset(mprev, 0.0))
            eyeb = eye.unsqueeze(1).broadcast_to([P, MH, P])
            bc = lambda x: x.unsqueeze(2).broadcast_to([P, MH, P])
            four = lambda x: x.rearrange("p (h n) -> p h n", h=MH)
            for c in range(2):
                a_c = g_a[:, 4 * c:4 * c + 4]
                E.op(v.tensor_tensor(DG, eyeb, bc(a_c), ALU.mult), "diag_a")
                E.wait("a_rows")
                step(v.tensor_tensor(TM, four(bank[3][:]), cst[:, C_PT:C_PT + P].unsqueeze(1).broadcast_to([P, MH, P]), ALU.add))
                step(v.tensor_reduce(cm, TM, AX, ALU.max))
                step(v.tensor_tensor(bc8[:, 0:4], cm, mprev, ALU.max))
                E.op(v.tensor_copy(bc8[:, 4:8], g_b[:, 4 * c:4 * c + 4]))
                E.op(v.tensor_tensor(DG, eyeb, bc(bc8[:, 0:4]), ALU.mult), "mm_diag")
                E.wait("m_rows")
                E.op(v.tensor_tensor(WT, cst[:, C_PS:C_PS + P].unsqueeze(1).broadcast_to([P, MH, P]), four(bank[3][:]), ALU.subtract))
                E.op(v.tensor_tensor(ex[:, 0:4], mprev, bc8[:, 0:4], ALU.subtract))
                E.op(v.scalar_tensor_tensor(ex[:, 4:8], bc8[:, 4:8], -1.0, bc8[:, 0:4], ALU.mult, ALU.subtract))
                E.wait("last_row")
                E.op(v.tensor_tensor(ex[:, 8:12], a_c, bank[0][:, 16:20], ALU.subtract))
                E.op(v.tensor_tensor(ex[:, 12:16], mprev, bank[0][:, 16:20], ALU.subtract))
                step(v.tensor_copy(mnew, bank[0][:, 16:20]))
                E.op(v.tensor_tensor(mnew, mnew, bank[0][:, 20:24], ALU.add), "ex_args")
                E.wait("wt_ready")
                E.wait("ex_ready")
                E.wait("kq")
                E.op(v.tensor_tensor(ST, four(bank[2][:]), WT, ALU.mult), "st_ready")
                E.op(v.tensor_tensor(WV, four(NAT[:, c, N:2 * N]), bc(ex[:, 8:12]), ALU.mult), "wv_ready")
                mo = MIXv[:, c, N:2 * N]
                E.wait("intra")
                if c == 0:
                    E.wait("og_ready")
                    step(v.tensor_copy(den, bank[0][:, 24:28]))
                    num = four(bank[6][:])
                else:
                    E.op(v.tensor_tensor(TM, four(bank[5][:]), bc(ex[:, 0:4]), ALU.mult))
                    step(v.tensor_tensor(den, bank[0][:, 28:32], ex[:, 0:4], ALU.mult))
                    E.op(v.tensor_tensor(TM, TM, four(bank[6][:]), ALU.add))
                    step(v.tensor_tensor(den, den, bank[0][:, 24:28], ALU.add))
                    num = TM
                step(v.scalar_tensor_tensor(den, den, -1.0, den, ALU.mult, ALU.max))
                step(v.tensor_tensor(den, den, ex[:, 4:8], ALU.max))
                E.op(v.reciprocal(den, den))
                step(v.tensor_tensor(four(mo), four(mo), num, ALU.mult))
                E.op(v.tensor_tensor(four(mo), four(mo), bc(den), ALU.mult))
                E.wait("state_mm")
                if c == 0:
                    E.op(v.tensor_copy(CT, four(bank[1][:])))
                    E.op(v.tensor_copy(nst, bank[2][:, 0:4]))
                else:
                    E.op(v.tensor_tensor(CT, CT, bc(ex[:, 12:16]), ALU.mult))
                    step(v.tensor_tensor(nst, nst, ex[:, 12:16], ALU.mult))
                    E.op(v.tensor_tensor(CT, CT, four(bank[1][:]), ALU.add))
                    E.op(v.tensor_tensor(nst, nst, bank[2][:, 0:4], ALU.add))
                step(v.tensor_copy(mprev, mnew), "chunk_done")

            lf8, i8 = g_lf[0:NB, 8:12], G3[0:NB, 2, 0:4]
            S = sE[0:NB, :]
            step(v.tensor_tensor(S[:, 0:4], lf8, smst[0:NB, 8:12], ALU.add))
            step(v.tensor_tensor(sM[0:NB, :], S[:, 0:4], i8, ALU.max))
            E.op(v.tensor_tensor(S[:, 4:8], i8, sM[0:NB, :], ALU.subtract))
            E.op(v.tensor_scalar(S[:, 8:12], sM[0:NB, :], -1.0, None, ALU.mult))
            step(v.tensor_tensor(S[:, 0:4], S[:, 0:4], sM[0:NB, :], ALU.subtract), "sE_args")
            E.wait("sE_ready")
            h8 = lambda x: x.rearrange("p (h n) -> p h n", h=MH)
            b4 = lambda x: x.unsqueeze(2).broadcast_to([NB, MH, P])
            E.op(v.tensor_tensor(KQW.rearrange("p (b h) -> p b h", b=NB), S[:, 0:4].unsqueeze(1).broadcast_to([NB, NB, MH]),
                                 eye8.unsqueeze(2).broadcast_to([NB, NB, MH]), ALU.mult), "smem_in")
            E.op(v.tensor_tensor(h8(EV), h8(SN[0:NB, 1536:2048]), b4(S[:, 4:8]), ALU.mult), "smem_in")
            q.wait_ge(sems("ns_in"), 16)
            E.wait("kqn_out")
            T8 = SN[0:NB, 512:1024]
            step(v.tensor_tensor(h8(NS), h8(NS), b4(S[:, 0:4]), ALU.mult))
            step(v.tensor_tensor(h8(T8), h8(KQN[:, 0:N]), b4(S[:, 4:8]), ALU.mult))
            step(v.tensor_tensor(NS, NS, T8, ALU.add))
            step(v.tensor_tensor(T8, NS, KQN[:, N:2 * N], ALU.mult))
            step(v.tensor_reduce(den[0:NB, :], h8(T8), AX, ALU.add))
            step(v.scalar_tensor_tensor(den[0:NB, :], den[0:NB, :], -1.0, den[0:NB, :], ALU.mult, ALU.max))
            step(v.tensor_tensor(den[0:NB, :], den[0:NB, :], S[:, 8:12], ALU.max))
            step(v.reciprocal(den[0:NB, :], den[0:NB, :]))
            E.wait("smem_mm")
            E.op(v.tensor_copy(wcB, bank[5][:, 0:32]))
            E.wait("smem_mm")
            step(v.tensor_copy(evT, bank[6][:, 0:32]), "ev_out")
            q.wait_ge(sems("cs_in"), 16)
            for b in range(NB):
                C = CS[:, b, :, :]
                E.wait("kq_rows")
                E.op(v.tensor_tensor(C, C, wcB[:, 4 * b:4 * b + 4].unsqueeze(2).broadcast_to([P, MH, P]), ALU.mult))
                step(v.tensor_tensor(T4, four(bank[KQ_BANKS[b % 2][0]][:]), evT[:, b:b + 25:8].unsqueeze(2).broadcast_to([P, MH, P]), ALU.mult))
                step(v.tensor_tensor(C, C, T4, ALU.add))
                step(v.tensor_tensor(T4, C, four(bank[KQ_BANKS[b % 2][1]][:]), ALU.mult), "kq_used")
                step(v.tensor_reduce(numS[:, b:b + 25:8], T4, AX, ALU.add))
            q.sem_inc(sems("c_new"), 1)
            q.wait_ge(sems("kv_used"), 34)
            for e in range(2):
                E.op(v.tensor_tensor(VO[:, e, :].rearrange("p (h d) -> p h d", h=AH),
                                     bank[7 - 3 * e][:].rearrange("p (h d) -> p h d", h=AH),
                                     cst[:, C_OWN:C_OWN + AH].unsqueeze(2).broadcast_to([P, AH, AD]), ALU.mult),
                     "vo_ready" if e else None)
            step(v.tensor_tensor(ri8[0:NB, :], ri8[0:NB, :], pn[0:NB, :], ALU.add))
            E.op(v.reciprocal(ri8[0:NB, :], ri8[0:NB, :]))
            at8 = MIX[0:NB, 2048:2560].rearrange("p (h d) -> p h d", h=AH)
            b8 = lambda x: x[0:NB, :].unsqueeze(2).broadcast_to([NB, AH, AD])
            step(v.tensor_tensor(at8, SN[0:NB, 1024:1536].rearrange("p (h d) -> p h d", h=AH), b8(pn), ALU.mult))
            E.wait("gate_mm")
            step(v.tensor_tensor(at8, at8, bank[6][0:NB, :].rearrange("p (h d) -> p h d", h=AH), ALU.add))
            step(v.tensor_tensor(at8, at8, b8(ri8), ALU.mult))
            E.wait("smem_mm")
            o8 = MIX[0:NB, 2560:3072]
            step(v.tensor_tensor(o8, o8, bank[5][0:NB, :], ALU.mult))
            step(v.tensor_tensor(h8(o8), h8(o8), b4(den[0:NB, :]), ALU.mult))
            q.sem_inc(sems("smem_done"), 1)

            q.wait_ge(sems("ln1_in"), 80)
            E.wait("mixT_out", 2)
            E.op(v.memset(QT[:, PH, :, 64:P], 0.0), "qt_zero")
            for t in range(3):
                E.wait("y_mm", 1 if t < 2 else 2)
                rows = P if t < 2 else NB
                sl = slice(0, rows)
                vec = lambda n, col: GV[sl, n * DM:(n + 1) * DM] if t < 2 else MOD[sl, col:col + DM]
                x, y, h2 = Xv[sl, t, :], MIXv[sl, t, :], H2[sl, t, :]
                g1 = vec(0, 2 * DM)
                for e in range(2):
                    E.op(v.tensor_tensor(y[:, e * N:(e + 1) * N], bank[2 * e + t if t < 2 else 6 + e][sl, :], g1[:, e * N:(e + 1) * N], ALU.mult))
                E.sync()
                step(v.scalar_tensor_tensor(y, x, ALPHA, y, ALU.mult, ALU.add))
                norm_rows(E, t, y, rows, y)
                E.sync()
                step(v.tensor_tensor(y, y, RA[sl, 0:DM], ALU.mult))
                step(v.tensor_tensor(x, y, RA[sl, DM:2 * DM], ALU.add))
                norm_rows(E, t, x, rows, h2)
                E.sync()
                step(v.scalar_tensor_tensor(h2, vec(1, 4 * DM), 1.0, h2, ALU.add, ALU.mult))
                E.op(v.tensor_tensor(h2, h2, vec(2, 3 * DM), ALU.add), "h2_ready")

            E.op(v.memset(MIX[0:NB, 2048:2560], 0.0), "zeros_ready")
            q.sem_inc(sems("u_slot_free"), UR)
            q.sem_inc(sems("diag_w"), 2 * PK)
            q.sem_inc(sems("scores_used"), 1)
            E.tally(("made", "u_slot_free")).n = UR
            E.tally(("made", "scores_used")).n = 1
            E.tally(("seen", "v_slot_free")).n = UR - PK
            E.tally(("seen", "scores")).n = 1

            def topk(par, first=False):
                E.wait("scores")
                E.hold()
                half_s = [bank[0][:, e * P:(e + 1) * P] for e in range(2)]
                lo = lambda e: slice(e * PK, e * PK + 8)
                hi = lambda e: slice(e * PK + 8, e * PK + 16)
                for e in range(2):
                    E.op(v.max(v2[:, lo(e)], half_s[e]))
                E.sync()
                E.hold()
                for e in range(2):
                    E.op(v.match_replace(TMPS[:, e * P:(e + 1) * P], v2[:, lo(e)], half_s[e], -3e38))
                E.sync()
                E.hold()
                for e in range(2):
                    E.op(v.max(v2[:, hi(e)], TMPS[:, e * P:(e + 1) * P]))
                for e in range(2):
                    E.op(v.max_index(ixu[:, lo(e)], v2[:, lo(e)], half_s[e]), "scores_used" if e else None)
                E.sync()
                E.hold()
                for e in range(2):
                    E.op(v.max_index(ixu[:, hi(e)], v2[:, hi(e)], TMPS[:, e * P:(e + 1) * P]))
                cand3 = CAND.rearrange("p (i j) -> p i j", i=PK)
                step(v.tensor_tensor(cand3, v2[:, 0:PK].unsqueeze(2).broadcast_to([P, PK, PK]),
                                     v2[:, PK:2 * PK].unsqueeze(1).broadcast_to([P, PK, PK]), ALU.add))
                E.op(v.tensor_copy(i2f, ixu[:, 0:2 * PK]))
                b_ = bs[par]
                E.sync()
                E.hold()
                step(v.max(b_[:, 0:8], CAND))
                E.hold()
                E.op(v.match_replace(CAND2, b_[:, 0:8], CAND, -3e38))
                E.op(v.max_index(ixu[:, 2 * PK:2 * PK + 8], b_[:, 0:8], CAND))
                E.sync()
                E.hold()
                step(v.max(b_[:, 8:16], CAND2))
                E.op(v.tensor_scalar(nbs[par], b_[:, 0:1], -1.0, None, ALU.mult), "best_ready")
                step(v.max_index(ixu[:, 2 * PK + 8:3 * PK], b_[:, 8:16], CAND2))
                E.op(v.tensor_scalar(ixu[:, 3 * PK:4 * PK], ixu[:, 2 * PK:3 * PK], 4, None, ALU.logical_shift_right))
                step(v.tensor_scalar(ixu[:, 4 * PK:5 * PK], ixu[:, 2 * PK:3 * PK], 15, None, ALU.bitwise_and))
                step(v.tensor_copy(abf, ixu[:, 3 * PK:5 * PK]))
                OH3 = OH.rearrange("p (s c) -> p s c", c=PK)
                step(v.tensor_tensor(OH3, cst[:, C_IOTA:C_IOTA + PK].unsqueeze(1).broadcast_to([P, 2 * PK, PK]),
                                     abf.unsqueeze(2).broadcast_to([P, 2 * PK, PK]), ALU.is_equal))
                OH4 = OH.rearrange("p (s k c) -> p s k c", s=2, c=PK)
                step(v.tensor_tensor(OH4, OH4, i2f.rearrange("p (s c) -> p s c", s=2).unsqueeze(2).broadcast_to([P, 2, PK, PK]), ALU.mult))
                step(v.tensor_reduce(selk, OH3, AX, ALU.add))
                if not first:
                    E.wait("v_slot_free", PK)
                step(v.scalar_tensor_tensor(tok[:, par * PK:(par + 1) * PK], selk[:, 0:PK], float(NK), selk[:, PK:2 * PK],
                                            ALU.mult, ALU.add), "idx_ready")

            def head(par, rows, h2, base, i=None):
                w = wS[par][0:rows, :]
                for k in range(PK):
                    s = k % UR
                    count = 16 * (base + k // UR + 1)
                    q.wait_ge(sems(f"u{s}_in"), count if i is None else i * 64 + count)
                    u = ring_t[0:rows, u_col(s):u_col(s) + DM]
                    E.op(v.tensor_tensor_reduce(out=u, in0=u, in1=h2, scale=1.0, scalar=0.0, op0=ALU.mult, op1=ALU.add,
                                                accum_out=w[:, k:k + 1]), "u_slot_free")
                E.sync()
                x, y = wA[0:rows, :], wB[0:rows, :]
                step(v.tensor_tensor(x, w, w, ALU.mult))
                step(v.tensor_scalar(x, x, 0.044715, 1.0, ALU.mult, ALU.add))
                step(v.tensor_tensor(y, x, w, ALU.mult))
                step(v.tensor_scalar(y, y, -2.0 * GC, 80.0, ALU.mult, ALU.min), "gelu_arg")
                E.wait("best_exp")
                step(v.reciprocal(er[0:rows, :], esum[par][0:rows, :]))
                step(v.tensor_scalar(x, ebs[par][0:rows, :], er[0:rows, :], None, ALU.mult))
                step(v.tensor_tensor(x, x, w, ALU.mult))
                E.wait("gelu_exp")
                step(v.tensor_scalar(y, y, 1.0, None, ALU.add))
                step(v.reciprocal(y, y))
                E.wait("diag_w", PK)
                E.op(v.tensor_tensor(wG[par][0:rows, :], x, y, ALU.mult), "w_ready")

            def finish(t):
                rows = P if t < 2 else NB
                sl = slice(0, rows)
                q.wait_ge(sems("ln2_in"), 48)
                E.wait("f_ready")
                g2 = RA[sl, 2048:3072] if t < 2 else MOD[sl, 5 * DM:6 * DM]
                x, y = Xv[sl, t, :], SN[sl, 0:DM]
                for e in range(2):
                    E.op(v.tensor_tensor(y[:, e * N:(e + 1) * N], bank[(4, 6, 2)[t] + e][sl, :], g2[:, e * N:(e + 1) * N], ALU.mult))
                E.sync()
                step(v.scalar_tensor_tensor(y, x, ALPHA, y, ALU.mult, ALU.add))
                norm_rows(E, t, y, rows, y, None, "var2_ready", "rstd2_ready")
                E.sync()
                step(v.tensor_tensor(y, y, RA[sl, 0:DM], ALU.mult))
                step(v.tensor_tensor(x, y, RA[sl, DM:2 * DM], ALU.add))
                q.sem_inc(sems("y_ready"), 1)

            topk(0, True)
            for t in range(NT):
                with E.loop(TRIPS[t], seen__scores=2, made__scores_used=2, made__best_ready=2, made__idx_ready=2,
                            seen__v_slot_free=2 * PK, made__u_slot_free=2 * PK, made__gelu_arg=2, seen__best_exp=2,
                            seen__gelu_exp=2, seen__diag_w=2 * PK, made__w_ready=2, made__dve_steps=60) as i:
                    for e in range(2):
                        head(e ^ t, P, H2[:, t, :], BASE[t] + 2 * e, i)
                        topk(1 - (e ^ t))
                if t == 0:
                    head(0, AH * NB, RA[0:AH * NB, 5120:6144], 2 * PH)
                    topk(1)
                    finish(0)
            finish(2)
            head(1, P, H2[:, 1, :], BASE[1] + 4 * TRIPS[1])
            topk(0)
            head(0, P, H2[:, 1, :], BASE[1] + 4 * TRIPS[1] + 2)
            finish(1)


INS = ["x_prompt", "x_sample", "cache_k", "cache_v", "page_table", "state_C", "state_n", "state_m", "state_conv",
       "c_prompt", "c_sample", "rel_bias_table", "w_ada", "b_ada", "w_in", "b_gate", "conv_w", "conv_b",
       "beta_attn", "beta_mlstm", "w_out", "ln1_g", "ln1_b", "w_query", "sub_keys", "expert_u", "expert_v",
       "ln2_g", "ln2_b"]
OUTS = [("y_prompt", (1, SEQ, DM)), ("y_sample", (NB, 1, DM)),
        ("k_prompt", (1, 1, SEQ, AH, AD)), ("v_prompt", (1, 1, SEQ, AH, AD)),
        ("C_prompt", (1, 1, MH, MD, MD)), ("n_prompt", (1, 1, MH, MD)), ("m_prompt", (1, 1, MH)),
        ("conv_prompt", (1, 1, CW - 1, 2 * MW)),
        ("k_sample", (1, NB, 1, AH, AD)), ("v_sample", (1, NB, 1, AH, AD)),
        ("C_sample", (1, NB, MH, MD, MD)), ("n_sample", (1, NB, MH, MD)), ("m_sample", (1, NB, MH)),
        ("conv_sample", (1, NB, CW - 1, 2 * MW))]


def kernel(**inputs):
    import concourse.bacc as bacc
    from concourse.bass_utils import run_bass_kernel_spmd

    nc = bacc.Bacc("TRN2", target_bir_lowering=False, num_devices=1)
    arrays = {n: np.ascontiguousarray(inputs[n]) for n in INS}
    arrays["consts"], arrays["onehot"] = constants()
    A = {n: nc.dram_tensor(f"in_{n}", a.shape, mybir.dt.from_np(a.dtype), kind="ExternalInput").ap() for n, a in arrays.items()}
    O = {n: nc.dram_tensor(f"out_{n}", s, F32, kind="ExternalOutput").ap() for n, s in OUTS}
    build(nc, A, O)
    r = run_bass_kernel_spmd(nc, [{f"in_{n}": a for n, a in arrays.items()}], core_ids=[0])
    return tuple(r.results[0][f"out_{n}"] for n, _ in OUTS)
```
